# Optimizing a Trainium2 kernel written in Bass

```python
import jax, jax.numpy as jnp
from jax import lax
import numpy as np

D_MODEL = 1024
BATCH = 1
SEQ = 256
DEPTH = 1

CHUNK = 64
MEM_LEN = 256
CONV_DIM = D_MODEL
CONV_WIDTH = 3
SB_HEADS = 16
SB_HEAD_DIM = 64
SB_DIM = SB_HEADS * SB_HEAD_DIM
SB_BLOCK = 128
X_HEADS = 4
X_HEAD_DIM = 256
X_DIM = X_HEADS * X_HEAD_DIM
N_BRANCH = 3
D_FF = 4 * D_MODEL
EPS = 1e-6

IN_SPLITS = [CONV_DIM, CONV_DIM, CONV_DIM, SB_DIM, SB_DIM, SB_DIM, X_DIM, N_BRANCH * D_MODEL]
IN_COLS = int(sum(IN_SPLITS))


def rms_norm(x, g):
    xf = x.astype(jnp.float32)
    y = xf * lax.rsqrt(jnp.mean(xf * xf, axis=-1, keepdims=True) + EPS)
    return (y * g.astype(jnp.float32)).astype(x.dtype)

def causal_depthwise_conv(u, w):
    c = u.shape[-1]
    return lax.conv_general_dilated(
        u, w.astype(u.dtype)[:, None, :], window_strides=(1,),
        padding=[(CONV_WIDTH - 1, 0)],
        dimension_numbers=("NWC", "WIO", "NWC"),
        feature_group_count=c)

def stick_breaking_attention(q, k, v):
    seq = q.shape[2]
    scale = q.shape[-1] ** -0.5
    outs = []
    for start in range(0, seq, SB_BLOCK):
        end = start + SB_BLOCK
        qb = q[:, :, start:end]
        kb = k[:, :, :end]
        vb = v[:, :, :end]
        z = jnp.einsum("bhqd,bhkd->bhqk", qb, kb).astype(jnp.float32) * scale
        t_idx = start + jnp.arange(SB_BLOCK)[:, None]
        s_idx = jnp.arange(end)[None, :]
        past = s_idx < t_idx
        log_beta = jax.nn.log_sigmoid(z)
        log_1mb = jnp.where(past, jax.nn.log_sigmoid(-z), 0.0)
        between = lax.cumsum(log_1mb, axis=3, reverse=True) - log_1mb
        a = jnp.where(past, jnp.exp(log_beta + between), 0.0)
        outs.append(jnp.einsum("bhqk,bhkd->bhqd", a.astype(vb.dtype), vb))
    return jnp.concatenate(outs, axis=2)

def memory_cross_attention(xq, mem_n, w_mem_kv, q_norm_g, k_norm_g):
    b, s, _ = xq.shape
    m = mem_n.shape[1]
    q = xq.reshape(b, s, X_HEADS, X_HEAD_DIM)
    kv = mem_n @ w_mem_kv
    k, v = jnp.split(kv, 2, axis=-1)
    k = k.reshape(b, m, X_HEADS, X_HEAD_DIM)
    v = v.reshape(b, m, X_HEADS, X_HEAD_DIM)
    q = rms_norm(q, q_norm_g)
    k = rms_norm(k, k_norm_g)
    scores = jnp.einsum("bqhd,bkhd->bhqk", q, k).astype(jnp.float32) * (X_HEAD_DIM ** -0.5)
    p = jax.nn.softmax(scores, axis=-1).astype(v.dtype)
    o = jnp.einsum("bhqk,bkhd->bqhd", p, v)
    return o.reshape(b, s, X_DIM)

def first_inputs(seed: int = 0) -> dict:
    key = jax.random.key(seed)
    ks = jax.random.split(key, 20)
    f32 = jnp.float32

    def nrm(k, shape, fan_in):
        return jax.random.normal(k, shape, f32) * (fan_in ** -0.5)

    def gain(k, shape):
        return 1.0 + 0.02 * jax.random.normal(k, shape, f32)

    L = DEPTH
    return {
        "x": jax.random.normal(ks[0], (BATCH, SEQ, D_MODEL), f32),
        "mem": jax.random.normal(ks[1], (BATCH, MEM_LEN, D_MODEL), f32),
        "g_mix": gain(ks[2], (L, D_MODEL)),
        "g_mem": gain(ks[3], (L, D_MODEL)),
        "w_in": nrm(ks[4], (L, D_MODEL, IN_COLS), D_MODEL),
        "conv_w": nrm(ks[5], (L, CONV_WIDTH, CONV_DIM), CONV_WIDTH),
        "w_conv_out": nrm(ks[6], (L, CONV_DIM, D_MODEL), CONV_DIM),
        "w_sb_out": nrm(ks[7], (L, SB_DIM, D_MODEL), SB_DIM),
        "q_norm_g": gain(ks[8], (L, X_HEAD_DIM)),
        "k_norm_g": gain(ks[9], (L, X_HEAD_DIM)),
        "w_mem_kv": nrm(ks[10], (L, D_MODEL, 2 * X_DIM), D_MODEL),
        "w_x_out": nrm(ks[11], (L, X_DIM, D_MODEL), X_DIM),
        "w_out": nrm(ks[12], (L, D_MODEL, D_MODEL), D_MODEL),
        "g_mlp": gain(ks[13], (L, D_MODEL)),
        "w_up": nrm(ks[14], (L, D_MODEL, D_FF), D_MODEL),
        "w_down": nrm(ks[15], (L, D_FF, D_MODEL), D_FF),
    }

def first_block(x, mem, g_mix, g_mem, w_in, conv_w, w_conv_out, w_sb_out, q_norm_g,
              k_norm_g, w_mem_kv, w_x_out, w_out, g_mlp, w_up, w_down):
    b, s, d = x.shape
    split_idx = list(np.cumsum(IN_SPLITS)[:-1])
    for l in range(DEPTH):
        h = rms_norm(x, g_mix[l])
        proj = h @ w_in[l]
        c_h, c_b, c_c, sq, sk, sv, xq, gate_pre = jnp.split(proj, split_idx, axis=-1)

        y_conv = (c_b * causal_depthwise_conv(c_c * c_h, conv_w[l])) @ w_conv_out[l]

        to_heads = lambda t: t.reshape(b, s, SB_HEADS, SB_HEAD_DIM).transpose(0, 2, 1, 3)
        o_sb = stick_breaking_attention(to_heads(sq), to_heads(sk), to_heads(sv))
        y_sb = o_sb.transpose(0, 2, 1, 3).reshape(b, s, SB_DIM) @ w_sb_out[l]

        mem_n = rms_norm(mem, g_mem[l])
        y_x = memory_cross_attention(xq, mem_n, w_mem_kv[l], q_norm_g[l], k_norm_g[l]) @ w_x_out[l]

        gates = jax.nn.sigmoid(gate_pre.astype(jnp.float32)).astype(x.dtype)
        gates = gates.reshape(b, s, N_BRANCH, d)
        merged = gates[:, :, 0] * y_conv + gates[:, :, 1] * y_sb + gates[:, :, 2] * y_x
        x = x + merged @ w_out[l]

        h2 = rms_norm(x, g_mlp[l])
        x = x + jnp.square(jax.nn.relu(h2 @ w_up[l])) @ w_down[l]
    return x


DEPTH_2 = 2

FOX_HEADS = 8
FOX_HEAD_DIM = 64
FOX_WIDTH = FOX_HEADS * FOX_HEAD_DIM
RET_HEADS = 4
RET_HEAD_DIM = 128
RET_WIDTH = RET_HEADS * RET_HEAD_DIM
MIX_WIDTH = FOX_WIDTH + RET_WIDTH
IN_COLS_2 = 3 * FOX_WIDTH + FOX_HEADS + 4 * RET_WIDTH
D_FF_2 = 4 * D_MODEL
Q_BLOCK = 128
RET_CHUNK = 128
ROPE_BASE = 10000.0
LN_EPS = 1e-5
GN_EPS = 1e-5
DEEPNORM_ALPHA = (2 * DEPTH_2) ** 0.25
DEEPNORM_BETA = (8 * DEPTH_2) ** -0.25


SPLITS = [FOX_WIDTH, 2 * FOX_WIDTH, 3 * FOX_WIDTH, 3 * FOX_WIDTH + FOX_HEADS,
          3 * FOX_WIDTH + FOX_HEADS + RET_WIDTH, 3 * FOX_WIDTH + FOX_HEADS + 2 * RET_WIDTH,
          3 * FOX_WIDTH + FOX_HEADS + 3 * RET_WIDTH]

def layernorm(x, g, b):
    xf = x.astype(jnp.float32)
    mu = jnp.mean(xf, axis=-1, keepdims=True)
    var = jnp.mean(jnp.square(xf - mu), axis=-1, keepdims=True)
    y = (xf - mu) * lax.rsqrt(var + LN_EPS)
    return (y * g + b).astype(x.dtype)

def rotary(x):
    s, d = x.shape[1], x.shape[-1]
    half = d // 2
    inv_freq = ROPE_BASE ** (-jnp.arange(half, dtype=jnp.float32) / half)
    ang = jnp.arange(s, dtype=jnp.float32)[:, None] * inv_freq[None, :]
    cos = jnp.cos(ang)[None, :, None, :]
    sin = jnp.sin(ang)[None, :, None, :]
    x1, x2 = x[..., :half].astype(jnp.float32), x[..., half:].astype(jnp.float32)
    return jnp.concatenate([x1 * cos - x2 * sin, x1 * sin + x2 * cos], axis=-1).astype(x.dtype)

def fox_attention(q, k, v, log_f):
    b, s, h, d = q.shape
    n_blocks = s // Q_BLOCK
    scale = d ** -0.5
    c = jnp.cumsum(log_f.astype(jnp.float32), axis=1).transpose(0, 2, 1)
    qb = q.reshape(b, n_blocks, Q_BLOCK, h, d).transpose(1, 0, 2, 3, 4)
    cb = c.reshape(b, h, n_blocks, Q_BLOCK).transpose(2, 0, 1, 3)
    key_pos = jnp.arange(s)

    def block(args):
        i, q_i, c_i = args
        scores = jnp.einsum('bqhd,bkhd->bhqk', q_i, k).astype(jnp.float32) * scale
        bias = c_i[..., :, None] - c[..., None, :]
        q_pos = i * Q_BLOCK + jnp.arange(Q_BLOCK)
        causal = key_pos[None, :] <= q_pos[:, None]
        logits = jnp.where(causal, scores + bias, -jnp.inf)
        p = jax.nn.softmax(logits, axis=-1)
        return jnp.einsum('bhqk,bkhd->bqhd', p.astype(v.dtype), v)

    out = lax.map(block, (jnp.arange(n_blocks), qb, cb))
    return out.transpose(1, 0, 2, 3, 4).reshape(b, s, h * d)

def retention_chunkwise(q, k, v, gamma):
    b, s, h, dk = q.shape
    dv = v.shape[-1]
    n_chunks = s // RET_CHUNK
    log_g = jnp.log(gamma)
    idx = jnp.arange(RET_CHUNK, dtype=jnp.float32)
    diff = idx[:, None] - idx[None, :]
    decay_mask = jnp.where(diff >= 0,
                           jnp.exp(log_g[:, None, None] * jnp.maximum(diff, 0.0)), 0.0)
    xi = jnp.exp(log_g[:, None] * (idx + 1.0))[..., None]
    zeta = jnp.exp(log_g[:, None] * (RET_CHUNK - 1.0 - idx))[..., None]
    chunk_decay = jnp.exp(log_g * RET_CHUNK)[:, None, None]

    def to_chunks(t):
        return t.reshape(b, n_chunks, RET_CHUNK, h, t.shape[-1]).transpose(1, 0, 3, 2, 4)

    def step(state, inp):
        q_i, k_i, v_i = inp
        inner = jnp.einsum('bhqd,bhkd->bhqk', q_i, k_i) * decay_mask
        o = (jnp.einsum('bhqk,bhkv->bhqv', inner, v_i)
             + jnp.einsum('bhqd,bhdv->bhqv', q_i * xi, state))
        state = chunk_decay * state + jnp.einsum('bhkd,bhkv->bhdv', k_i * zeta, v_i)
        return state, o

    state0 = jnp.zeros((b, h, dk, dv), jnp.float32)
    _, out = lax.scan(step, state0, (to_chunks(q), to_chunks(k), to_chunks(v)))
    return out.transpose(1, 0, 3, 2, 4).reshape(b, s, h, dv)

def head_groupnorm(x, g):
    xf = x.astype(jnp.float32)
    mu = jnp.mean(xf, axis=-1, keepdims=True)
    var = jnp.mean(jnp.square(xf - mu), axis=-1, keepdims=True)
    return ((xf - mu) * lax.rsqrt(var + GN_EPS) * g).astype(x.dtype)

def hybrid_layer(x, w_in, w_out, w_ff1, w_ff2, ln1_g, ln1_b, ln2_g, ln2_b, b_forget, ret_gn_g, gamma):
    b, s, _ = x.shape
    proj = jnp.einsum('bsd,dc->bsc', x, w_in)
    fq, fk, fv, f_logit, rq, rk, rv, rg = jnp.split(proj, SPLITS, axis=-1)

    fshape = (b, s, FOX_HEADS, FOX_HEAD_DIM)
    log_f = jax.nn.log_sigmoid((f_logit + b_forget).astype(jnp.float32))
    fox_out = fox_attention(fq.reshape(fshape), fk.reshape(fshape), fv.reshape(fshape), log_f)

    rshape = (b, s, RET_HEADS, RET_HEAD_DIM)
    q_r = rotary(rq.reshape(rshape))
    k_r = rotary(rk.reshape(rshape)) * (RET_HEAD_DIM ** -0.5)
    ret = retention_chunkwise(q_r, k_r, rv.reshape(rshape), gamma)
    ret = head_groupnorm(ret, ret_gn_g).reshape(b, s, RET_WIDTH).astype(x.dtype)
    ret_out = jax.nn.silu(rg) * ret

    mixed = jnp.concatenate([fox_out.astype(x.dtype), ret_out], axis=-1)
    mix = jnp.einsum('bsc,cd->bsd', mixed, w_out)
    x = layernorm(DEEPNORM_ALPHA * x + mix, ln1_g, ln1_b)

    hid = jnp.square(jax.nn.relu(jnp.einsum('bsd,df->bsf', x, w_ff1)))
    ff = jnp.einsum('bsf,fd->bsd', hid, w_ff2)
    return layernorm(DEEPNORM_ALPHA * x + ff, ln2_g, ln2_b)

def second_inputs(seed: int = 0) -> dict:
    key = jax.random.key(seed)
    ks = jax.random.split(key, 12)
    f32 = jnp.float32
    x = jax.random.normal(ks[0], (BATCH, SEQ, D_MODEL), f32)
    w_in = jax.random.normal(ks[1], (DEPTH_2, D_MODEL, IN_COLS_2), f32) * D_MODEL ** -0.5
    col = jnp.arange(IN_COLS_2)
    is_value = (((col >= SPLITS[1]) & (col < SPLITS[2]))
                | ((col >= SPLITS[5]) & (col < SPLITS[6])))
    w_in = w_in * jnp.where(is_value, DEEPNORM_BETA, 1.0).astype(f32)
    w_out = jax.random.normal(ks[2], (DEPTH_2, MIX_WIDTH, D_MODEL), f32) * (MIX_WIDTH ** -0.5 * DEEPNORM_BETA)
    w_ff1 = jax.random.normal(ks[3], (DEPTH_2, D_MODEL, D_FF_2), f32) * (D_MODEL ** -0.5 * DEEPNORM_BETA)
    w_ff2 = jax.random.normal(ks[4], (DEPTH_2, D_FF_2, D_MODEL), f32) * (D_FF_2 ** -0.5 * DEEPNORM_BETA)
    ln1_g = 1.0 + 0.02 * jax.random.normal(ks[5], (DEPTH_2, D_MODEL), f32)
    ln1_b = 0.02 * jax.random.normal(ks[6], (DEPTH_2, D_MODEL), f32)
    ln2_g = 1.0 + 0.02 * jax.random.normal(ks[7], (DEPTH_2, D_MODEL), f32)
    ln2_b = 0.02 * jax.random.normal(ks[8], (DEPTH_2, D_MODEL), f32)
    b_forget = jax.random.uniform(ks[9], (DEPTH_2, FOX_HEADS), f32, 1.0, 5.0)
    ret_gn_g = 1.0 + 0.02 * jax.random.normal(ks[10], (DEPTH_2, RET_HEADS, RET_HEAD_DIM), f32)
    return {"x": x, "w_in": w_in, "w_out": w_out, "w_ff1": w_ff1, "w_ff2": w_ff2,
            "ln1_g": ln1_g, "ln1_b": ln1_b, "ln2_g": ln2_g, "ln2_b": ln2_b,
            "b_forget": b_forget, "ret_gn_g": ret_gn_g}

def second_block(x, w_in, w_out, w_ff1, w_ff2, ln1_g, ln1_b, ln2_g, ln2_b, b_forget, ret_gn_g):
    gamma = 1.0 - jnp.exp2(-5.0 - jnp.arange(RET_HEADS, dtype=jnp.float32))
    for layer in range(DEPTH_2):
        x = hybrid_layer(x, w_in[layer], w_out[layer], w_ff1[layer], w_ff2[layer],
                         ln1_g[layer], ln1_b[layer], ln2_g[layer], ln2_b[layer],
                         b_forget[layer], ret_gn_g[layer], gamma)
    return x


def setup_inputs(seed=0):
    out = dict(first_inputs(seed))
    for name, value in second_inputs(seed + 1).items():
        if name != "x":
            out[name + "_2"] = value
    return out


def reference(
    x, mem, g_mix, g_mem, w_in, conv_w, w_conv_out, w_sb_out, q_norm_g, k_norm_g, w_mem_kv,
    w_x_out, w_out, g_mlp, w_up, w_down, w_in_2, w_out_2, w_ff1_2, w_ff2_2, ln1_g_2, ln1_b_2,
    ln2_g_2, ln2_b_2, b_forget_2, ret_gn_g_2,
):
    x = first_block(
        x, mem, g_mix, g_mem, w_in, conv_w, w_conv_out, w_sb_out, q_norm_g, k_norm_g, w_mem_kv,
        w_x_out, w_out, g_mlp, w_up, w_down,
    )
    return second_block(
        x, w_in_2, w_out_2, w_ff1_2, w_ff2_2, ln1_g_2, ln1_b_2, ln2_g_2, ln2_b_2, b_forget_2,
        ret_gn_g_2,
    )


_drawn_inputs = setup_inputs


def setup_inputs(seed=0):
    import zlib

    import numpy as np

    out = dict(_drawn_inputs(seed))
    spreads = {}
    factors = {'g_mix': 2.689,
     'g_mem': 8.0,
     'q_norm_g': 8.0,
     'k_norm_g': 8.0,
     'g_mlp': 3.034,
     'ret_gn_g_2': 8.0}
    for name, (base, spread) in spreads.items():
        noise = np.random.default_rng([zlib.crc32(name.encode()), seed]).standard_normal(out[name].shape)
        drawn = base * np.exp(spread * noise) if base else spread * noise
        out[name] = __import__('jax').numpy.asarray(drawn.astype(out[name].dtype))
    for name, factor in factors.items():
        out[name] = (out[name] * factor).astype(out[name].dtype)
    return out
```

```python
import numpy as np
import concourse.bass as bass
from concourse import mybir
from contextlib import ExitStack


F32 = mybir.dt.float32
F32R = mybir.dt.float32r
ALU = mybir.AluOpType
ACT = mybir.ActivationFunctionType
AX = mybir.AxisListType

P = 128
D = 1024
T = 256
KT = D // P
FF = 4 * D
HALF = KT * 256
LAYERS = 2
EPS_RMS, EPS_LN, EPS_GN = 1e-6, 1e-5, 1e-5
ALPHA = (2 * LAYERS) ** 0.25

SQ, SK, SV, CC, CH, CB, MK, MV, XQ = range(0, 36, 4)
GATED = {"sb": 36, "x": 44, "conv": 52}
WO1 = 60
FFN1 = 64
HALVES1 = 96
LF, LFQ, LFK, LFV, LRQ, LRK, LRV, LRG, LWO, LFFN = 0, 2, 4, 6, 8, 10, 12, 14, 16, 20
HALVES2 = 52
EVACS1, EVACS2 = 64, 19
FOX_HEADS, RET_HEADS = 8, 4
SB_PAIRS, X_HEADS = 8, 4

G_MIX, G_MEM, G_MLP, G_Q, G_K, CONVW = 0, 8, 16, 24, 26, 28
PARAMS1 = 52
LN1_G, LN1_B, LN2_G, LN2_B, GN_G, B_F = 0, 8, 16, 24, 32, 36
PARAMS2 = 44
C_ID, C_GT, C_LE, C_ONE, C_PAST, C_EPS, CONSTS1 = 0, 128, 256, 384, 512, 640, 644
C_COS, C_SIN, C_DECAY, C_ROT, C_CAUSAL, CONSTS2 = 0, 256, 512, 1536, 1664, 2048

ACT_STEPS_LAYER = 6
DVE_STEPS_LAYER = 42


class Steps:

    def __init__(self, eng, sem, base=0):
        self.eng, self.sem, self.base, self.n = eng, sem, base, 0

    def mark(self, ins):
        ins.then_inc(self.sem, 1)
        self.n += 1

    def settle(self):
        self.eng.wait_ge(self.sem, self.base + self.n)


def build(nc, mem_t, x_t, w1, w2, wf, par1, par2, con1, con2, out_t):
    with ExitStack() as ctx:
        def sb(name, shape, dt=F32):
            return ctx.enter_context(nc.sbuf_tensor(name, shape, dt))

        def sem(name):
            return ctx.enter_context(nc.semaphore(name))

        raw = sb("raw", [P, 2, HALF])
        w_hi = sb("w_hi", [P, 4, HALF], F32R)
        w_lo = sb("w_lo", [P, 4, HALF], F32R)
        H_hi, H_lo = sb("H_hi", [P, KT, T], F32R), sb("H_lo", [P, KT, T], F32R)
        R_hi, R_lo = sb("R_hi", [P, KT, T], F32R), sb("R_lo", [P, KT, T], F32R)
        Q_hi, Q_lo = sb("Q_hi", [P, KT, T], F32R), sb("Q_lo", [P, KT, T], F32R)
        B1, B2, B3 = (sb(f"B{i}", [P, KT, T]) for i in (1, 2, 3))
        B4 = sb("B4", [P, KT, T + 2])
        B5, B6, B7 = (sb(f"B{i}", [P, KT, T]) for i in (5, 6, 7))
        spb = sb("spb", [P, 2, 2, 384])
        soft = sb("soft", [P, 2, 384])
        staged = sb("staged", [P, 2, 512])
        sqh = sb("sqh", [P, 2, 512])
        rs = sb("rs", [P, 3, T])
        cst = sb("cst", [P, CONSTS1])
        par = sb("par", [P, PARAMS1])
        lpar = sb("lpar", [P, PARAMS2])
        small = sb("small", [P, 4, 16])
        fgate = sb("fgate", [P, 2, 16])

        ident, gt = cst[:, C_ID:C_ID + P], cst[:, C_GT:C_GT + P]
        le_one = cst[:, C_LE:C_LE + 2 * P]
        le, ones = cst[:, C_LE:C_LE + P], cst[:, C_ONE:C_ONE + P]
        past = cst[:, C_PAST:C_PAST + P]
        one_col = cst[:, C_ONE:C_ONE + 1]
        eps_rms, eps_ln = cst[:, C_EPS:C_EPS + 1], cst[:, C_EPS + 1:C_EPS + 2]

        qs, ks = B1, B2
        vs = B3[:, :, :].rearrange("p a t -> p (a t)").rearrange("p (m n) -> p m n", m=2)
        u, y = B4, B5
        kx, qx = B6, B7
        vx = B4[:, :, :].rearrange("p a t -> p (a t)")[:, 0:2 * D].rearrange("p (m n) -> p m n", m=2)
        merged, ox = B1, B3
        b5 = B5[:, :, :].rearrange("p a t -> p (a t)")
        xp, xpt = b5[:, 0:512].rearrange("p (m n) -> p m n", m=2), b5[:, 512:1024]
        gate = b5[:, 1024:2048].rearrange("p (m n) -> p m n", m=2)
        X = B2
        hid_s = spb[:, :, :, :].rearrange("p a b t -> p (a b t)")[:, 0:1024].rearrange(
            "p (a n) -> p a n", a=2)
        fq, fk = B1[:, 0:4, :], B1[:, 4:8, :]
        b3 = B3[:, :, :].rearrange("p a t -> p (a t)")
        fv = b3[:, 0:1024].rearrange("p (m n) -> p m n", m=2)
        rv = b3[:, 1024:2048].rearrange("p (m n) -> p m n", m=2)
        b4 = B4[:, :, :].rearrange("p a t -> p (a t)")
        inner = b4[:, 0:1536].rearrange("p (h n) -> p h n", h=4)
        rott = b4[:, 1536:2048].rearrange("p (h n) -> p h n", h=2)
        rq, rk = B5[:, 0:4, :], B5[:, 4:8, :]
        rg, ro = B6[:, 0:4, :], B6[:, 4:8, :]
        gsq, gr0 = B1[:, 0:4, :], B1[:, 4:8, :]
        gv, ga = B5[:, 0:4, :], B5[:, 4:8, :]
        rsig = sqh[:, :, :].rearrange("p a n -> p (a n)").rearrange("p (h n) -> p h n", h=4)
        con = B7[:, :, :].rearrange("p a t -> p (a t)")
        cos_b = con[:, C_COS:C_COS + T].unsqueeze(1).to_broadcast([P, 2, T])
        sin_b = con[:, C_SIN:C_SIN + T].unsqueeze(1).to_broadcast([P, 2, T])
        decay = con[:, C_DECAY:C_DECAY + 4 * T].rearrange("p (h n) -> p h n", h=4)
        rot = con[:, C_ROT:C_ROT + P]
        causal = con[:, C_CAUSAL:C_CAUSAL + 384]
        fm = soft
        fl = spb[:, 0, :, :]
        fpt = spb[:, 1, :, :]

        gps = ctx.enter_context(nc.psum_tensor("gps", [P, 4, 512], F32))
        aps = ctx.enter_context(nc.psum_tensor("aps", [P, 4, 512], F32))

        raw_loaded = [sem("raw_loaded0"), sem("raw_loaded1")]
        names = """in_loaded x_loaded par_loaded con_loaded lpar_loaded out_stored
            hi_ready lo_ready gemm_done evac act_step dve_step act_step2 dve_step2 pads
            nsq nsum nvar nlog nrow nt nhi nlo nmean ncent nres resid
            staged_free conv_y cv_hi cv_lo
            sb_z sb_sp sb_soft sb_lb sb_t sb_arg sb_e sb_a sb_o sb_ohi sb_olo
            hn_sum hn_var hn_log hn_row hn_norm
            cx_s cx_max cx_exp cx_p cx_t cx_pt cx_o cx_oe ox_hi ox_lo
            mg mg_hi mg_lo ffn_relu ffn_sq ffn_hi hidden
            f_logit f_sp f_log f_m fx_s fx_l fx_max fx_e fx_p fx_t fx_pt fx_o fx_ohi fx_oe
            rt_mm rt_x rn_s rn_m rn_o rn_oe gn_mean gn_c gn_sq gn_var gn_v gn_log gn_y gn_hi gn_lo""".split()
        s = {n: sem(n) for n in names}
        block = ctx.enter_context(nc.Block())

        def raw_slot(l):
            return l % 2

        def ring(l):
            return l % 4

        def raw_count(h0, l):
            return h0 * 8 + (l // 2 + 1) * 16

        @block.sync
        def _(sp):
            def load(h0, l, src, first=False, n=HALF):
                if not first:
                    sp.wait_ge(s["lo_ready"], h0 + (l - 1))
                sp.dma_start(raw[:, raw_slot(l), 0:n], src).then_inc(raw_loaded[raw_slot(l)], 16)

            sp.dma_start(B6[:, :, :], x_t.rearrange("(k p) t -> p k t", p=P)).then_inc(s["in_loaded"], 16)
            sp.dma_start(par[:, :], par1).then_inc(s["par_loaded"], 16)
            sp.dma_start(cst[:, :], con1).then_inc(s["par_loaded"], 16)
            load(0, 0, w1[0], first=True)
            load(0, 1, w1[1], first=True)
            sp.dma_start(B7[:, :, :], mem_t.rearrange("(k p) t -> p k t", p=P)).then_inc(s["in_loaded"], 16)
            with sp.Fori(0, 14) as i:
                for a in range(2):
                    sp.wait_ge(s["lo_ready"], i * 2 + a + 1)
                    sp.dma_start(raw[:, a, :], w1[i * 2 + a + 2]).then_inc(raw_loaded[a], 16)
            sp.wait_ge(s["sb_z"], SB_PAIRS)
            sp.dma_start(X[:, :, :], x_t.rearrange("(k p) t -> p k t", p=P)).then_inc(s["x_loaded"], 16)
            with sp.Fori(0, (HALVES1 - 30) // 2) as i:
                for a in range(2):
                    sp.wait_ge(s["lo_ready"], i * 2 + a + 29)
                    sp.dma_start(raw[:, a, :], w1[i * 2 + a + 30]).then_inc(raw_loaded[a], 16)
            sp.wait_ge(s["cx_s"], X_HEADS)
            sp.dma_start(con, con2).then_inc(s["con_loaded"], 16)
            with sp.Fori(0, LAYERS) as ly:
                h0 = ly * HALVES2 + HALVES1
                sp.wait_ge(s["nlo"], ly * 8 + 16)
                sp.dma_start(lpar[:, :], par2[ly]).then_inc(s["lpar_loaded"], 16)
                load(h0, 0, wf[ly, 0], n=32)
                load(h0, 1, wf[ly, 1], n=32)
                with sp.Fori(0, 25) as i:
                    for a in range(2):
                        sp.wait_ge(s["lo_ready"], h0 + i * 2 + (a + 1))
                        sp.dma_start(raw[:, a, :], w2[ly, i * 2 + a]).then_inc(raw_loaded[a], 16)
            sp.wait_ge(s["nres"], 4 * 2 * LAYERS)
            sp.dma_start(out_t.rearrange("(k p) t -> p k t", p=P), X[:, :, :]).then_inc(s["out_stored"], 16)
            sp.wait_ge(s["out_stored"], 16)

        @block.scalar
        def _(act):
            st = Steps(act, s["act_step"])

            def split(h0, l, n=HALF, start=False):
                act.wait_ge(raw_loaded[raw_slot(l)], raw_count(h0, l))
                if not start:
                    act.wait_ge(s["gemm_done"], h0 + (l - 3))
                act.activation(w_hi[:, ring(l), 0:n], raw[:, raw_slot(l), 0:n], ACT.Copy)\
                   .then_inc(s["hi_ready"], 1)

            def bank(l, ringsize=3):
                return gps[:, l % ringsize, :]

            def two(ap):
                return ap.rearrange("p (a t) -> p a t", a=2)

            def evac(dst, src, done, scale=1.0):
                act.wait_ge(s["gemm_done"], done)
                act.activation(dst, src, ACT.Copy, scale=scale).then_inc(s["evac"], 1)

            def rsqrt_start(v, tmp, r0, done):
                st.mark(act.activation(tmp, v, ACT.Ln))
                st.settle()
                act.activation(r0, tmp, ACT.Exp, scale=-0.5).then_inc(done, 1)

            def norm(i, si, src, sq, nbuf, hi, ln=None, cent=0, res=0):
                for a in range(2):
                    if ln is not None:
                        act.wait_ge(s["ncent"], cent + a + 1)
                    act.activation(sq[:, 4 * a:4 * a + 4, 0:T], src[:, 4 * a:4 * a + 4, :], ACT.Square)\
                       .then_inc(s["nsq"], 1)
                act.wait_ge(s["nvar"], i + 1)
                rsqrt_start(rs[:, 2, :], rs[:, 0, :], rs[:, 1, :], s["nlog"])
                for q in range(4):
                    act.wait_ge(s["nt"], i * 4 + (q + 1))
                    if ln is not None:
                        for k in (2 * q, 2 * q + 1):
                            ins = act.activation(src[:, k, :], nbuf[:, k, 0:T], ACT.Identity,
                                                 bias=lpar[:, ln + k:ln + k + 1])
                        ins.then_inc(s["nres"], 1)
                        act.wait_ge(s["nres"], res + q + 1)
                    fr = nbuf if ln is None else src
                    act.activation(hi[:, 2 * q:2 * q + 2, :], fr[:, 2 * q:2 * q + 2, 0:T], ACT.Copy)\
                       .then_inc(s["nhi"], 1)

            def up(h, l, uu, par_, a, fresh=False):
                act.wait_ge(s["gemm_done"], h + (l + 1))
                if not fresh:
                    act.wait_ge(s["ffn_sq"], uu - 1)
                act.activation(staged[:, a, :], gps[:, 2 * par_ + a, :], ACT.Relu)\
                   .then_inc(s["ffn_relu"], 1)
                act.wait_ge(s["ffn_relu"], uu + 1)
                t0 = 4 * par_ + 2 * a
                act.activation(Q_hi[:, t0:t0 + 2, :], two(staged[:, a, :]), ACT.Square)\
                   .then_inc(s["ffn_hi"], 1)

            def ffn(h0, l0, ub, first=False):
                for a in range(2):
                    split(h0, l0 + 4 + a)
                    up(h0, l0 + a, ub + a, 0, a, fresh=first)
                with act.Fori(0, 3) as f:
                    hf, uf = h0 + f * 8, ub + f * 4
                    for a in range(2):
                        split(hf, l0 + 6 + a)
                        up(hf, l0 + 2 + a, uf + (2 + a), 1, a)
                    split(hf, l0 + 8)
                    split(hf, l0 + 9)
                    for a in range(2):
                        split(hf, l0 + 10 + a)
                        up(hf, l0 + 6 + a, uf + (4 + a), 0, a)
                    split(hf, l0 + 12)
                    split(hf, l0 + 13)
                for a in range(2):
                    split(h0, l0 + 30 + a)
                    up(h0, l0 + 26 + a, ub + (14 + a), 1, a)

            def sb_out(i):
                act.wait_ge(s["sb_o"], i + 1)
                act.activation(Q_hi[:, i, :], aps[:, 2, 0:T], ACT.Copy).then_inc(s["sb_ohi"], 1)

            def sb_softplus(i):
                act.wait_ge(s["sb_z"], i + 1)
                if i >= 2:
                    act.wait_ge(s["sb_o"], i - 1)
                b = spb[:, i % 2, :, :]
                st.mark(act.activation(b, aps[:, 0:2, 0:384], ACT.Abs))
                st.settle()
                st.mark(act.activation(b, b, ACT.Exp, scale=-1.0))
                st.settle()
                act.activation(b, b, ACT.Ln, bias=one_col).then_inc(s["sb_sp"], 1)

            def sb_exp(i):
                act.wait_ge(s["sb_arg"], i + 1)
                b = spb[:, i % 2, :, :]
                act.activation(b, b, ACT.Exp).then_inc(s["sb_e"], 1)

            def head_rsqrt(n):
                act.wait_ge(s["hn_var"], n + 1)
                rsqrt_start(rs[:, 2, :], rs[:, 0, :], rs[:, 1, :], s["hn_log"])

            def cx_out(h):
                act.wait_ge(s["cx_o"], h + 1)
                act.activation(ox[:, 2 * h:2 * h + 2, :], two(aps[:, 2, :]), ACT.Copy)\
                   .then_inc(s["cx_oe"], 1)

            def cx_copy(h):
                act.wait_ge(s["cx_t"], h + 1)
                if h >= 1:
                    act.wait_ge(s["cx_o"], h)
                act.activation(xpt, aps[:, 3, :], ACT.Copy).then_inc(s["cx_pt"], 1)

            def cx_exp(h):
                act.wait_ge(s["cx_max"], h + 1)
                if h >= 1:
                    act.wait_ge(s["cx_t"], h)
                for t in range(2):
                    act.activation(xp[:, t, :], aps[:, h % 2, t * T:(t + 1) * T], ACT.Exp,
                                   bias=small[:, 1, 2 * h + t:2 * h + t + 1], scale=1.0 / 16,
                                   accum_out=small[:, 2, 2 * h + t:2 * h + t + 1]).then_inc(s["cx_exp"], 1)

            act.preload_act_table_set("natural_log_exp_and_others")
            act.wait_ge(s["in_loaded"], 16)
            act.wait_ge(s["par_loaded"], 32)
            norm(0, 0, B6, B5, B1, H_hi)
            for l in range(4):
                split(0, l, start=True)
            staged_n = 0
            for h in range(FFN1):
                if h + 4 < HALVES1:
                    split(0, h + 4)
                ps = bank(h)
                if h < SK:
                    i = h - SQ
                    evac(qs[:, 2 * i:2 * i + 2, :], two(ps), h + 1, scale=0.125)
                elif h < SV:
                    i = h - SK
                    evac(ks[:, 2 * i:2 * i + 2, :], two(ps), h + 1)
                elif h < CC:
                    i = h - SV
                    evac(vs[:, :, 256 * i:256 * i + 256], two(ps), h + 1)
                elif h < CH:
                    i = h - CC
                    evac(u[:, 2 * i:2 * i + 2, 2:T + 2], two(ps), h + 1)
                elif h < MK:
                    if staged_n >= 2:
                        act.wait_ge(s["staged_free"], staged_n - 1)
                    evac(staged[:, staged_n % 2, :], ps, h + 1)
                    staged_n += 1
                elif h < MV or XQ <= h < XQ + 4:
                    n = h - MK if h < MV else 4 + h - XQ
                    i = n % 4
                    act.wait_ge(s["gemm_done"], h + 1)
                    dst = kx if n < 4 else qx
                    act.activation(dst[:, 2 * i:2 * i + 2, :], two(ps), ACT.Copy)
                    if n >= 2:
                        act.wait_ge(s["hn_sum"], n - 1)
                    act.activation(sqh[:, n % 2, :], ps, ACT.Square).then_inc(s["evac"], 1)
                elif h < XQ:
                    i = h - MV
                    evac(vx[:, :, 256 * i:256 * i + 256], two(ps), h + 1)
                elif h < WO1:
                    if (h - 36) % 2 == 0:
                        act.wait_ge(s["gemm_done"], h + 1)
                        act.wait_ge(s["staged_free"], staged_n - 1)
                        act.activation(gate[:, staged_n % 2, :], ps, ACT.Sigmoid).then_inc(s["evac"], 1)
                    else:
                        act.wait_ge(s["staged_free"], staged_n - 1)
                        evac(staged[:, staged_n % 2, :], ps, h + 1)
                        staged_n += 1
                        if h > GATED["conv"]:
                            i = (h - GATED["conv"]) // 2
                            act.wait_ge(s["mg"], i + 1)
                            act.activation(Q_hi[:, 2 * i:2 * i + 2, :], merged[:, 2 * i:2 * i + 2, :],
                                           ACT.Copy).then_inc(s["mg_hi"], 1)
                else:
                    act.wait_ge(s["staged_free"], staged_n - 1)
                    evac(staged[:, staged_n % 2, :], ps, h + 1)
                    staged_n += 1
                if h == 1:
                    act.wait_ge(s["in_loaded"], 32)
                    norm(1, 1, B7, B5, B4, R_hi)
                if h >= 12 and h % 2 == 0 and h <= 30:
                    t = (h - 12) // 2
                    if t >= 2:
                        sb_out(t - 2)
                    if t < SB_PAIRS:
                        sb_softplus(t)
                    if 1 <= t <= SB_PAIRS:
                        sb_exp(t - 1)
                if MK + 1 <= h <= MK + 4 or XQ + 1 <= h <= XQ + 4:
                    head_rsqrt(h - MK - 1 if h < XQ else 4 + h - XQ - 1)
                if XQ <= h < XQ + 4:
                    i = h - XQ
                    act.wait_ge(s["gemm_done"], XQ)
                    act.wait_ge(s["conv_y"], i + 1)
                    act.activation(R_hi[:, 2 * i:2 * i + 2, :], y[:, 2 * i:2 * i + 2, :], ACT.Copy)\
                       .then_inc(s["cv_hi"], 1)
                if h == XQ + 3:
                    act.wait_ge(s["cv_lo"], 4)
                x0 = XQ + 3
                if x0 + 2 <= h < x0 + 2 + X_HEADS:
                    cx_out(h - x0 - 2)
                if x0 + 1 <= h < x0 + 1 + X_HEADS:
                    cx_copy(h - x0 - 1)
                if x0 <= h < x0 + X_HEADS:
                    cx_exp(h - x0)
                if h == GATED["x"] - 1:
                    act.wait_ge(s["gemm_done"], h + 1)
                    for i in range(4):
                        act.activation(Q_hi[:, 2 * i:2 * i + 2, :], ox[:, 2 * i:2 * i + 2, :], ACT.Copy)\
                           .then_inc(s["ox_hi"], 1)
            act.preload_act_table_set("natural_log_exp_and_others")
            act.wait_ge(s["resid"], 4)
            norm(2, 2, X, B5, B1, R_hi)
            act.wait_ge(s["staged_free"], staged_n)
            ffn(0, FFN1, 0, first=True)
            for q in range(4):
                act.wait_ge(s["resid"], 4 + q + 1)
                act.activation(H_hi[:, 2 * q:2 * q + 2, :], X[:, 2 * q:2 * q + 2, :], ACT.Copy)\
                   .then_inc(s["nhi"], 1)

            with act.Fori(0, LAYERS) as ly:
                st = Steps(act, s["act_step2"], ly * ACT_STEPS_LAYER)
                h0 = ly * HALVES2 + HALVES1
                e0 = ly * EVACS2 + EVACS1

                def fox_softplus():
                    act.wait_ge(s["f_logit"], ly + 1)
                    fa = small[:, 0, :]
                    st.mark(act.activation(fa, fgate[:, 0, :], ACT.Abs))
                    st.settle()
                    st.mark(act.activation(fa, fa, ACT.Exp, scale=-1.0))
                    st.settle()
                    act.activation(fa, fa, ACT.Ln, bias=one_col).then_inc(s["f_sp"], 1)

                def fox_out(c):
                    act.wait_ge(s["fx_o"], ly * 8 + (2 * c + 2))
                    act.activation(Q_hi[:, c, :], aps[:, 3, 0:T], ACT.Copy).then_inc(s["fx_ohi"], 1)

                def fox_copy(h):
                    act.wait_ge(s["fx_t"], ly * 8 + (h + 1))
                    act.activation(fpt[:, h % 2, :], aps[:, 2, 0:384], ACT.Copy).then_inc(s["fx_pt"], 1)

                def fox_exp(h):
                    act.wait_ge(s["fx_max"], ly * 8 + (h + 1))
                    for t, (c0, c1) in enumerate(((0, 128), (128, 384))):
                        act.activation(fl[:, h % 2, c0:c1], fl[:, h % 2, c0:c1], ACT.Exp,
                                       bias=small[:, 1, 2 * h + t:2 * h + t + 1],
                                       accum_out=small[:, 2, 2 * h + t:2 * h + t + 1])\
                           .then_inc(s["fx_e"], 1)

                for l in range(4):
                    split(h0, l, n=32 if l < 2 else HALF)
                for l in range(LFFN):
                    split(h0, l + 4)
                    ps = bank(l)
                    done = h0 + (l + 1)
                    a = l % 2
                    if l == LF:
                        pass
                    elif l == LF + 1:
                        act.wait_ge(s["gemm_done"], done)
                        act.activation(fgate[:, 0, :], gps[:, 1, 0:16], ACT.Copy).then_inc(s["evac"], 1)
                        fox_softplus()
                    elif l < LFK:
                        evac(fq[:, 2 * a:2 * a + 2, :], two(ps), done, scale=0.125)
                    elif l < LFV:
                        evac(fk[:, 2 * a:2 * a + 2, :], two(ps), done)
                    elif l < LRQ:
                        evac(fv[:, :, 256 * a:256 * a + 256], two(ps), done)
                    elif l < LRK:
                        evac(rq[:, 2 * a:2 * a + 2, :], two(ps), done)
                    elif l < LRV:
                        evac(rk[:, 2 * a:2 * a + 2, :], two(ps), done, scale=P ** -0.5)
                    elif l < LRG:
                        evac(rv[:, :, 256 * a:256 * a + 256], two(ps), done)
                    elif l < LWO:
                        act.wait_ge(s["gemm_done"], done)
                        act.activation(rg[:, 2 * a:2 * a + 2, :], two(ps), ACT.Copy)
                        act.activation(rsig[:, 2 * a:2 * a + 2, :], two(ps), ACT.Sigmoid)\
                           .then_inc(s["evac"], 1)
                    else:
                        act.wait_ge(s["staged_free"], ly * 4 + (24 + l - LWO - 1))
                        evac(staged[:, l % 2, :], ps, done)
                    if l >= 7 and l <= 14 and l % 2 == 0:
                        fox_out((l - 8) // 2)
                    if 6 <= l < 14:
                        fox_copy(l - 6)
                    if 5 <= l < 13:
                        fox_exp(l - 5)
                    if l == LRG + 1:
                        for b in range(2):
                            act.wait_ge(s["rn_o"], ly * 2 + (b + 1))
                            act.activation(ro[:, 2 * b:2 * b + 2, :], two(aps[:, b, :]), ACT.Copy)\
                               .then_inc(s["rn_oe"], 1)
                        for b in range(2):
                            act.wait_ge(s["gn_c"], ly * 2 + (b + 1))
                            act.activation(gsq[:, 2 * b:2 * b + 2, :], ro[:, 2 * b:2 * b + 2, :],
                                           ACT.Square).then_inc(s["gn_sq"], 1)
                        for b in range(2):
                            act.wait_ge(s["gn_v"], ly * 2 + (b + 1))
                            r0 = gr0[:, 2 * b:2 * b + 2, :]
                            rsqrt_start(gv[:, 2 * b:2 * b + 2, :], r0, r0, s["gn_log"])
                        for b in range(2):
                            act.wait_ge(s["gn_y"], ly * 2 + (b + 1))
                            act.activation(Q_hi[:, 4 + 2 * b:6 + 2 * b, :], ro[:, 2 * b:2 * b + 2, :],
                                           ACT.Copy).then_inc(s["gn_hi"], 1)
                norm(ly * 2 + 3, 0, X, B5, B1, R_hi, ln=LN1_B, cent=ly * 4, res=ly * 8)
                act.wait_ge(s["staged_free"], ly * 4 + 28)
                ffn(h0, LFFN, ly * 16 + 16)
                norm(ly * 2 + 4, 0, X, B5, B1, H_hi, ln=LN2_B, cent=ly * 4 + 2, res=ly * 8 + 4)
                assert st.n == ACT_STEPS_LAYER, st.n

        @block.vector
        def _(dve):
            st = Steps(dve, s["dve_step"])

            def split(h0, l, n=HALF):
                dve.wait_ge(s["hi_ready"], h0 + (l + 1))
                dve.tensor_tensor(w_lo[:, ring(l), 0:n], raw[:, raw_slot(l), 0:n],
                                  w_hi[:, ring(l), 0:n].bitcast(F32), ALU.subtract)\
                   .then_inc(s["lo_ready"], 1)

            def two(ap):
                return ap.rearrange("p (a t) -> p a t", a=2)

            def rsqrt(ps, scale, eps, v, r0, a, r, ready, log, count, done):
                dve.tensor_scalar(v, ps, scale, eps, ALU.mult, ALU.add).then_inc(ready, 1)
                dve.wait_ge(ready, count)
                dve.wait_ge(log, count)
                st.mark(dve.tensor_tensor(a, v, r0, ALU.mult))
                st.settle()
                st.mark(dve.tensor_tensor(a, a, r0, ALU.mult))
                st.settle()
                st.mark(dve.tensor_scalar(a, a, -0.5, 1.5, ALU.mult, ALU.add))
                st.settle()
                ins = dve.tensor_tensor(r, a, r0, ALU.mult)
                if done is None:
                    st.mark(ins)
                    st.settle()
                else:
                    ins.then_inc(done, 1)

            def norm(i, si, src, nbuf, hi, lo, g, ln=False):
                if ln:
                    dve.wait_ge(s["nmean"], i - 2)
                    for a in range(2):
                        t = src[:, 4 * a:4 * a + 4, :]
                        dve.scalar_tensor_tensor(
                            t, aps[:, 2, 0:T].unsqueeze(1).to_broadcast([P, 4, T]), -1.0 / D, t,
                            ALU.mult, ALU.add).then_inc(s["ncent"], 1)
                dve.wait_ge(s["nsum"], i + 1)
                rsqrt(aps[:, 3, 0:T], 1.0 / D, EPS_LN if ln else EPS_RMS, rs[:, 2, :], rs[:, 1, :],
                      rs[:, 0, :], rs[:, 2, :], s["nvar"], s["nlog"], i + 1, s["nrow"])
                dve.wait_ge(s["nrow"], i + 1)
                for q in range(4):
                    for k in (2 * q, 2 * q + 1):
                        ins = dve.scalar_tensor_tensor(nbuf[:, k, 0:T], src[:, k, :], g[:, k:k + 1],
                                                       rs[:, 2, :], ALU.mult, ALU.mult)
                    ins.then_inc(s["nt"], 1)
                for q in range(4):
                    dve.wait_ge(s["nhi"], si * 4 + (q + 1))
                    dve.tensor_tensor(lo[:, 2 * q:2 * q + 2, :],
                                      (src if ln else nbuf)[:, 2 * q:2 * q + 2, 0:T],
                                      hi[:, 2 * q:2 * q + 2, :].bitcast(F32), ALU.subtract)\
                       .then_inc(s["nlo"], 1)

            def up(uu, par_, a):
                t0 = 4 * par_ + 2 * a
                dve.wait_ge(s["ffn_relu"], uu + 1)
                dve.tensor_tensor(hid_s[:, a, :], staged[:, a, :], staged[:, a, :], ALU.mult)\
                   .then_inc(s["ffn_sq"], 1)
                dve.wait_ge(s["ffn_sq"], uu + 1)
                dve.wait_ge(s["ffn_hi"], uu + 1)
                dve.tensor_tensor(Q_lo[:, t0:t0 + 2, :], two(hid_s[:, a, :]),
                                  Q_hi[:, t0:t0 + 2, :].bitcast(F32), ALU.subtract)\
                   .then_inc(s["hidden"], 1)

            def ffn(h0, l0, ub, alpha):
                for a in range(2):
                    split(h0, l0 + 4 + a)
                    up(ub + a, 0, a)
                with dve.Fori(0, 3) as f:
                    hf, uf = h0 + f * 8, ub + f * 4
                    for a in range(2):
                        split(hf, l0 + 6 + a)
                        up(uf + (2 + a), 1, a)
                    split(hf, l0 + 8)
                    split(hf, l0 + 9)
                    for a in range(2):
                        split(hf, l0 + 10 + a)
                        up(uf + (4 + a), 0, a)
                    split(hf, l0 + 12)
                    split(hf, l0 + 13)
                for a in range(2):
                    split(h0, l0 + 30 + a)
                    up(ub + (14 + a), 1, a)
                for b in range(4):
                    if b % 2 == 0:
                        dve.wait_ge(s["gemm_done"], h0 + (l0 + 31 + b // 2))
                    t = X[:, 2 * b:2 * b + 2, :]
                    dve.scalar_tensor_tensor(t, t, alpha, two(aps[:, b, :]), ALU.mult, ALU.add)\
                       .then_inc(s["resid"], 1)

            diag2 = past.unsqueeze(1).to_broadcast([P, 2, P])

            def mask_diagonals(b, done):
                for hh in range(2):
                    t = b[:, hh, :].rearrange("p (c n) -> p c n", c=3)[:, 0:3:2, :]
                    ins = dve.tensor_tensor(t, t, diag2, ALU.mult)
                ins.then_inc(done, 1)

            def sb_out(i):
                dve.wait_ge(s["sb_ohi"], i + 1)
                dve.tensor_tensor(Q_lo[:, i, :], aps[:, 2, 0:T], Q_hi[:, i, :].bitcast(F32),
                                  ALU.subtract).then_inc(s["sb_olo"], 1)

            def sb_parts(i):
                b, z = spb[:, i % 2, :, :], aps[:, 0:2, 0:384]
                dve.wait_ge(s["sb_sp"], i + 1)
                if i >= 1:
                    dve.wait_ge(s["sb_t"], i)
                st.mark(dve.scalar_tensor_tensor(soft[:, :, :], z, 0.0, b, ALU.max, ALU.add))
                st.settle()
                mask_diagonals(soft, s["sb_soft"])
                dve.scalar_tensor_tensor(b, z, 0.0, b, ALU.min, ALU.subtract).then_inc(s["sb_lb"], 1)

            def sb_arg(i):
                b = spb[:, i % 2, :, :]
                dve.wait_ge(s["sb_t"], i + 1)
                dve.wait_ge(s["sb_lb"], i + 1)
                dve.tensor_tensor(b, b, aps[:, 2:4, 0:384], ALU.subtract).then_inc(s["sb_arg"], 1)

            def sb_mask(i):
                dve.wait_ge(s["sb_e"], i + 1)
                mask_diagonals(spb[:, i % 2, :, :], s["sb_a"])

            def head_norm(n):
                i = n % 4
                dst = kx if n < 4 else qx
                g = G_K if n < 4 else G_Q
                dve.wait_ge(s["hn_sum"], n + 1)
                if n >= 1:
                    dve.wait_ge(s["hn_norm"], n)
                rsqrt(gps[:, 3, 0:T], 1.0 / 256, EPS_RMS, rs[:, 2, :], rs[:, 1, :], rs[:, 0, :],
                      rs[:, 2, :], s["hn_var"], s["hn_log"], n + 1, s["hn_row"])
                dve.wait_ge(s["hn_row"], n + 1)
                for j in range(2):
                    t = dst[:, 2 * i + j, :]
                    ins = dve.scalar_tensor_tensor(t, t, par[:, g + j:g + j + 1], rs[:, 2, :],
                                                   ALU.mult, ALU.mult)
                ins.then_inc(s["hn_norm"], 1)

            def cx_max(h):
                dve.wait_ge(s["cx_s"], h + 1)
                st.mark(dve.tensor_reduce(small[:, 0, 2 * h:2 * h + 2], two(aps[:, h % 2, :]),
                                          AX.X, ALU.max))
                st.settle()
                dve.tensor_scalar(small[:, 1, 2 * h:2 * h + 2], small[:, 0, 2 * h:2 * h + 2],
                                  -1.0 / 16, None, ALU.mult).then_inc(s["cx_max"], 1)

            def cx_scale(h):
                dve.wait_ge(s["cx_exp"], 2 * h + 2)
                st.mark(dve.reciprocal(small[:, 3, 2 * h:2 * h + 2], small[:, 2, 2 * h:2 * h + 2]))
                st.settle()
                for t in range(2):
                    ins = dve.tensor_scalar(xp[:, t, :], xp[:, t, :],
                                            small[:, 3, 2 * h + t:2 * h + t + 1], None, ALU.mult)
                ins.then_inc(s["cx_p"], 1)

            dve.wait_ge(s["par_loaded"], 32)
            norm(0, 0, B6, B1, H_hi, H_lo, par[:, G_MIX:G_MIX + KT])
            for l in range(4):
                split(0, l)
            staged_n = 0
            for h in range(FFN1):
                split(0, h + 4)
                if CH <= h < MK:
                    dve.wait_ge(s["evac"], h + 1)
                    i = (h - CH) % 4
                    sg = two(staged[:, staged_n % 2, :])
                    staged_n += 1
                    if h < CB:
                        t = u[:, 2 * i:2 * i + 2, 2:T + 2]
                        dve.wait_ge(s["pads"], 1)
                        dve.tensor_tensor(t, t, sg, ALU.mult).then_inc(s["staged_free"], 1)
                        dve.wait_ge(s["staged_free"], staged_n)
                        for tap in (2, 1, 0):
                            for k in (2 * i, 2 * i + 1):
                                wc = par[:, CONVW + 8 * tap + k:CONVW + 8 * tap + k + 1]
                                if tap == 2:
                                    ins = dve.tensor_scalar(y[:, k, :], u[:, k, 2:T + 2], wc, None, ALU.mult)
                                else:
                                    ins = dve.scalar_tensor_tensor(y[:, k, :], u[:, k, tap:T + tap], wc,
                                                                   y[:, k, :], ALU.mult, ALU.add)
                            st.mark(ins)
                            st.settle()
                    else:
                        t = y[:, 2 * i:2 * i + 2, :]
                        dve.tensor_tensor(t, t, sg, ALU.mult).then_inc(s["staged_free"], 1)
                elif 36 <= h < WO1 and (h - 36) % 2 == 1:
                    i = (h - 36) // 2 % 4
                    dve.wait_ge(s["evac"], h + 1)
                    m = merged[:, 2 * i:2 * i + 2, :]
                    sg, gg = staged[:, staged_n % 2, :], gate[:, staged_n % 2, :]
                    staged_n += 1
                    if h < GATED["x"]:
                        dve.tensor_tensor(m, two(sg), two(gg), ALU.mult).then_inc(s["staged_free"], 1)
                    else:
                        st.mark(dve.tensor_tensor(sg, sg, gg, ALU.mult))
                        st.settle()
                        dve.tensor_tensor(m, m, two(sg), ALU.add).then_inc(s["staged_free"], 1)
                    if h > GATED["conv"]:
                        dve.wait_ge(s["staged_free"], staged_n)
                        dve.sem_inc(s["mg"], 1)
                        dve.wait_ge(s["mg_hi"], i + 1)
                        dve.tensor_tensor(Q_lo[:, 2 * i:2 * i + 2, :], m,
                                          Q_hi[:, 2 * i:2 * i + 2, :].bitcast(F32), ALU.subtract)\
                           .then_inc(s["mg_lo"], 1)
                elif h >= WO1:
                    i = h - WO1
                    dve.wait_ge(s["evac"], h + 1)
                    dve.wait_ge(s["x_loaded"], 16)
                    t = X[:, 2 * i:2 * i + 2, :]
                    dve.tensor_tensor(t, t, two(staged[:, staged_n % 2, :]), ALU.add)\
                       .then_inc(s["resid"], 1)
                    dve.wait_ge(s["resid"], i + 1)
                    dve.sem_inc(s["staged_free"], 1)
                    staged_n += 1
                if h == 1:
                    norm(1, 1, B7, B4, R_hi, R_lo, par[:, G_MEM:G_MEM + KT])
                    dve.wait_ge(s["nlo"], 8)
                    dve.memset(u[:, :, 0:2], 0.0).then_inc(s["pads"], 1)
                if h >= 12 and h % 2 == 0 and h <= 30:
                    t = (h - 12) // 2
                    if t >= 2:
                        sb_out(t - 2)
                    if t < SB_PAIRS:
                        sb_parts(t)
                    if 1 <= t <= SB_PAIRS:
                        sb_arg(t - 1)
                        sb_mask(t - 1)
                if MK + 1 <= h <= MK + 4 or XQ + 1 <= h <= XQ + 4:
                    head_norm(h - MK - 1 if h < XQ else 4 + h - XQ - 1)
                if XQ <= h < XQ + 4:
                    i = h - XQ
                    if i == 0:
                        dve.wait_ge(s["staged_free"], 8)
                        dve.sem_inc(s["conv_y"], 4)
                    dve.wait_ge(s["cv_hi"], i + 1)
                    dve.tensor_tensor(R_lo[:, 2 * i:2 * i + 2, :], y[:, 2 * i:2 * i + 2, :],
                                      R_hi[:, 2 * i:2 * i + 2, :].bitcast(F32), ALU.subtract)\
                       .then_inc(s["cv_lo"], 1)
                x0 = XQ + 3
                if x0 <= h < x0 + X_HEADS:
                    cx_max(h - x0)
                    cx_scale(h - x0)
                if h == GATED["x"] - 1:
                    for i in range(4):
                        dve.wait_ge(s["ox_hi"], i + 1)
                        dve.tensor_tensor(Q_lo[:, 2 * i:2 * i + 2, :], ox[:, 2 * i:2 * i + 2, :],
                                          Q_hi[:, 2 * i:2 * i + 2, :].bitcast(F32), ALU.subtract)\
                           .then_inc(s["ox_lo"], 1)
            norm(2, 2, X, B1, R_hi, R_lo, par[:, G_MLP:G_MLP + KT])
            ffn(0, FFN1, 0, 1.0)
            for q in range(4):
                dve.wait_ge(s["nhi"], 12 + q + 1)
                dve.tensor_tensor(H_lo[:, 2 * q:2 * q + 2, :], X[:, 2 * q:2 * q + 2, :],
                                  H_hi[:, 2 * q:2 * q + 2, :].bitcast(F32), ALU.subtract)\
                   .then_inc(s["nlo"], 1)
            dve.wait_ge(s["con_loaded"], 16)

            with dve.Fori(0, LAYERS) as ly:
                st = Steps(dve, s["dve_step2"], ly * DVE_STEPS_LAYER)
                h0 = ly * HALVES2 + HALVES1
                e0 = ly * EVACS2 + EVACS1
                f0 = ly * 8
                logf = fgate[:, 1, :]

                def forget(h):
                    if h >= 1:
                        dve.wait_ge(s["fx_s"], f0 + h)
                    m = fm[:, h % 2, :]
                    dve.tensor_scalar(m[:, 0:256], le_one, logf[:, h:h + 1], None, ALU.mult)
                    dve.tensor_scalar(m[:, 256:384], le, logf[:, 8 + h:9 + h], None, ALU.mult)\
                       .then_inc(s["f_m"], 1)

                def fox_max(h):
                    dve.wait_ge(s["fx_s"], f0 + (h + 1))
                    if h >= 2:
                        dve.wait_ge(s["fx_t"], f0 + (h - 1))
                    lg = fl[:, h % 2, :]
                    dve.tensor_tensor(lg, aps[:, h % 2, 0:384], causal, ALU.add).then_inc(s["fx_l"], 1)
                    dve.wait_ge(s["fx_l"], f0 + (h + 1))
                    dve.tensor_reduce(small[:, 3, 2 * h:2 * h + 1], lg[:, 0:128], AX.X, ALU.max)
                    st.mark(dve.tensor_reduce(small[:, 3, 2 * h + 1:2 * h + 2], lg[:, 128:384],
                                              AX.X, ALU.max))
                    st.settle()
                    dve.tensor_scalar(small[:, 1, 2 * h:2 * h + 2], small[:, 3, 2 * h:2 * h + 2],
                                      -1.0, None, ALU.mult).then_inc(s["fx_max"], 1)

                def fox_scale(h):
                    dve.wait_ge(s["fx_e"], ly * 16 + (2 * h + 2))
                    lg = fl[:, h % 2, :]
                    st.mark(dve.reciprocal(small[:, 3, 2 * h:2 * h + 2], small[:, 2, 2 * h:2 * h + 2]))
                    st.settle()
                    dve.tensor_scalar(lg[:, 0:128], lg[:, 0:128], small[:, 3, 2 * h:2 * h + 1],
                                      None, ALU.mult)
                    dve.tensor_scalar(lg[:, 128:384], lg[:, 128:384], small[:, 3, 2 * h + 1:2 * h + 2],
                                      None, ALU.mult).then_inc(s["fx_p"], 1)

                def fox_out(c):
                    dve.wait_ge(s["fx_ohi"], ly * 4 + (c + 1))
                    dve.tensor_tensor(Q_lo[:, c, :], aps[:, 3, 0:T], Q_hi[:, c, :].bitcast(F32),
                                      ALU.subtract).then_inc(s["fx_oe"], 1)

                def rotate(r):
                    x = (rq if r < 2 else rk)[:, 2 * (r % 2):2 * (r % 2) + 2, :]
                    dve.wait_ge(s["rt_mm"], ly * 4 + (r + 1))
                    st.mark(dve.tensor_tensor(rott, two(gps[:, 3, :]), sin_b, ALU.mult))
                    st.mark(dve.tensor_tensor(x, x, cos_b, ALU.mult))
                    st.settle()
                    dve.tensor_tensor(x, x, rott, ALU.add).then_inc(s["rt_x"], 1)

                for l in range(4):
                    split(h0, l, n=32 if l < 2 else HALF)
                for l in range(LFFN):
                    split(h0, l + 4)
                    if l == LF + 1:
                        dve.wait_ge(s["evac"], e0 + 1)
                        dve.wait_ge(s["lpar_loaded"], ly * 16 + 16)
                        fg = fgate[:, 0, :].rearrange("p (a h) -> p a h", a=2)
                        dve.tensor_tensor(fg, fg, lpar[:, B_F:B_F + 8].unsqueeze(1).to_broadcast([P, 2, 8]),
                                          ALU.add).then_inc(s["f_logit"], 1)
                        dve.wait_ge(s["f_logit"], ly + 1)
                        dve.wait_ge(s["f_sp"], ly + 1)
                        st.mark(dve.scalar_tensor_tensor(logf, fgate[:, 0, :], 0.0, small[:, 0, :],
                                                         ALU.min, ALU.subtract))
                        st.settle()
                    if l >= LWO:
                        i = l - LWO
                        dve.wait_ge(s["evac"], e0 + l)
                        t = X[:, 2 * i:2 * i + 2, :]
                        dve.scalar_tensor_tensor(t, t, ALPHA, two(staged[:, l % 2, :]), ALU.mult,
                                                 ALU.add).then_inc(s["resid"], 1)
                        dve.wait_ge(s["resid"], ly * 8 + (8 + i + 1))
                        dve.sem_inc(s["staged_free"], 1)
                    if l >= 7 and l <= 14 and l % 2 == 0:
                        fox_out((l - 8) // 2)
                    if l == 4:
                        forget(0)
                    if 5 <= l < 13:
                        fox_max(l - 5)
                        if l < 12:
                            forget(l - 4)
                        fox_scale(l - 5)
                    if 10 <= l < 14:
                        rotate(l - 10)
                    if l == LRG:
                        for h in range(RET_HEADS):
                            sc = (aps[:, h, :] if h < 3 else gps[:, 3, :])
                            dve.wait_ge(s["rn_s"], ly * 4 + (h + 1))
                            dve.tensor_tensor(inner[:, h, 0:256], sc[:, 0:256], decay[:, h, :], ALU.mult)
                            dve.tensor_tensor(inner[:, h, 256:384], sc[:, 256:384], decay[:, h, 0:128],
                                              ALU.mult).then_inc(s["rn_m"], 1)
                    if l == LRG + 1:
                        for b in range(2):
                            t = ro[:, 2 * b:2 * b + 2, :]
                            dve.wait_ge(s["gn_mean"], ly * 2 + (b + 1))
                            dve.scalar_tensor_tensor(t, two(aps[:, 2 + b, :]), -1.0 / P, t, ALU.mult,
                                                     ALU.add).then_inc(s["gn_c"], 1)
                        dve.wait_ge(s["evac"], e0 + LWO - 1)
                        st.mark(dve.tensor_tensor(rg, rg, rsig, ALU.mult))
                        st.settle()
                        for b in range(2):
                            dve.wait_ge(s["gn_var"], ly * 2 + (b + 1))
                            dve.wait_ge(s["gn_c"], ly * 2 + (b + 1))
                            rsqrt(two(aps[:, b, :]), 1.0 / P, EPS_GN, gv[:, 2 * b:2 * b + 2, :],
                                  gr0[:, 2 * b:2 * b + 2, :], ga[:, 2 * b:2 * b + 2, :],
                                  gv[:, 2 * b:2 * b + 2, :], s["gn_v"], s["gn_log"],
                                  ly * 2 + (b + 1), None)
                            for h in (2 * b, 2 * b + 1):
                                ins = dve.scalar_tensor_tensor(ro[:, h, :], ro[:, h, :],
                                                               lpar[:, GN_G + h:GN_G + h + 1],
                                                               gv[:, h, :], ALU.mult, ALU.mult)
                            st.mark(ins)
                            st.settle()
                            t = ro[:, 2 * b:2 * b + 2, :]
                            dve.tensor_tensor(t, t, rg[:, 2 * b:2 * b + 2, :], ALU.mult)\
                               .then_inc(s["gn_y"], 1)
                            dve.wait_ge(s["gn_y"], ly * 2 + (b + 1))
                        for b in range(2):
                            dve.wait_ge(s["gn_hi"], ly * 2 + (b + 1))
                            dve.tensor_tensor(Q_lo[:, 4 + 2 * b:6 + 2 * b, :], ro[:, 2 * b:2 * b + 2, :],
                                              Q_hi[:, 4 + 2 * b:6 + 2 * b, :].bitcast(F32), ALU.subtract)\
                               .then_inc(s["gn_lo"], 1)
                norm(ly * 2 + 3, ly * 2 + 4, X, B1, R_hi, R_lo, lpar[:, LN1_G:LN1_G + KT], ln=True)
                ffn(h0, LFFN, ly * 16 + 16, ALPHA)
                norm(ly * 2 + 4, ly * 2 + 5, X, B1, H_hi, H_lo, lpar[:, LN2_G:LN2_G + KT], ln=True)
                assert st.n == DVE_STEPS_LAYER, st.n

        @block.tensor
        def _(pe):
            def rows_first(h0, l, bank_, op_hi, op_lo, split_count=None):
                pe.wait_ge(s["lo_ready"], h0 + (l + 1))
                r = ring(l)
                for nt in range(2):
                    for k in range(KT):
                        if nt == 0 and k % 2 == 0 and split_count is not None:
                            pe.wait_ge(split_count[0], split_count[1] + (k // 2 + 1))
                        c = k * 256 + nt * P
                        out = gps[:, bank_, nt * T:(nt + 1) * T]
                        pe.matmul(out, w_hi[:, r, c:c + P], op_hi[:, k, :], start=(k == 0), stop=False)
                        pe.matmul(out, w_hi[:, r, c:c + P], op_lo[:, k, :], start=False, stop=False)
                        ins = pe.matmul(out, w_lo[:, r, c:c + P], op_hi[:, k, :], start=False,
                                        stop=(k == KT - 1))
                ins.then_inc(s["gemm_done"], 1)

            def tokens_first(h0, l, bank_, op_hi, op_lo):
                pe.wait_ge(s["lo_ready"], h0 + (l + 1))
                r = ring(l)
                for m in range(2):
                    for k in range(KT):
                        out = gps[:, bank_, m * 256:(m + 1) * 256]
                        wh, wl = w_hi[:, r, k * 256:(k + 1) * 256], w_lo[:, r, k * 256:(k + 1) * 256]
                        xh, xl = op_hi[:, k, m * P:(m + 1) * P], op_lo[:, k, m * P:(m + 1) * P]
                        pe.matmul(out, xh, wh, start=(k == 0), stop=False)
                        pe.matmul(out, xh, wl, start=False, stop=False)
                        ins = pe.matmul(out, xl, wh, start=False, stop=(k == KT - 1))
                ins.then_inc(s["gemm_done"], 1)

            def column_sums(src, out, ready=None, done=None):
                for k in range(KT):
                    if ready is not None and k % 4 == 0:
                        pe.wait_ge(ready[0], ready[1] + (k // 4 + 1))
                    ins = pe.matmul(out, ones, src[:, k, 0:T], start=(k == 0), stop=(k == KT - 1))
                ins.then_inc(done, 1)

            def ffn(h0, l0, ub, free, split_count):
                def up(h, l, par_, free_sem, free_count):
                    for a in range(2):
                        pe.wait_ge(free_sem, free_count + a)
                        rows_first(h, l + a, 2 * par_ + a, R_hi, R_lo,
                                   split_count if free_sem is not s["ffn_relu"] else None)

                def down(h, l, par_, uu, first=False, last=False):
                    pe.wait_ge(s["hidden"], uu)
                    for a in range(2):
                        pe.wait_ge(s["lo_ready"], h + (l + a + 1))
                        r = ring(l + a)
                        for nt in range(4):
                            out = aps[:, 2 * a + nt // 2, (nt % 2) * T:(nt % 2 + 1) * T]
                            for k in range(4):
                                c = k * 512 + nt * P
                                hh, hl = Q_hi[:, 4 * par_ + k, :], Q_lo[:, 4 * par_ + k, :]
                                pe.matmul(out, w_hi[:, r, c:c + P], hh,
                                          start=(first and k == 0 and nt % 2 == 0), stop=False,
                                          skip_group_check=True)
                                pe.matmul(out, w_hi[:, r, c:c + P], hl, start=False, stop=False,
                                          skip_group_check=True)
                                ins = pe.matmul(out, w_lo[:, r, c:c + P], hh, start=False,
                                                stop=(last and k == 3 and nt % 2 == 1),
                                                skip_group_check=True)
                        ins.then_inc(s["gemm_done"], 1)

                relu = s["ffn_relu"]
                for a in range(2):
                    rows_first(h0, l0 + a, a, R_hi, R_lo, split_count if a == 0 else None)
                for a in range(2):
                    rows_first(h0, l0 + 2 + a, 2 + a, R_hi, R_lo)
                down(h0, l0 + 4, 0, ub + 2, first=True)
                with pe.Fori(0, 3) as f:
                    hf, uf = h0 + f * 8, ub + f * 4
                    up(hf, l0 + 6, 0, relu, uf + 1)
                    down(hf, l0 + 8, 1, uf + 4)
                    up(hf, l0 + 10, 1, relu, uf + 3)
                    down(hf, l0 + 12, 0, uf + 6)
                down(h0, l0 + 30, 1, ub + 16, last=True)

            def sb_scores(i):
                if i >= 1:
                    pe.wait_ge(s["sb_lb"], i)
                for hh in range(2):
                    q, k = qs[64 * hh:64 * hh + 64, i, :], ks[64 * hh:64 * hh + 64, i, :]
                    pe.matmul(aps[:, hh, 0:256], k[:, 0:128], q, start=True, stop=True)
                    ins = pe.matmul(aps[:, hh, 256:384], k[:, 128:256], q[:, 128:256],
                                    start=True, stop=True)
                ins.then_inc(s["sb_z"], 1)

            def sb_between(i):
                pe.wait_ge(s["sb_soft"], i + 1)
                if i >= 1:
                    pe.wait_ge(s["sb_olo"], i)
                for hh in range(2):
                    pe.matmul(aps[:, 2 + hh, 0:384], gt, soft[:, hh, :], start=True, stop=False)
                    ins = pe.matmul(aps[:, 2 + hh, 128:256], ones, soft[:, hh, 256:384],
                                    start=False, stop=True)
                ins.then_inc(s["sb_t"], 1)

            def sb_values(i):
                pe.wait_ge(s["sb_a"], i + 1)
                for hh in range(2):
                    c = (2 * i + hh) * 64
                    a = spb[:, i % 2, hh, :]
                    out = aps[64 * hh:64 * hh + 64, 2, :]
                    pe.matmul(out[:, 0:256], vs[:, 0, c:c + 64], a[:, 0:256], start=True, stop=False)
                    ins = pe.matmul(out[:, 128:256], vs[:, 1, c:c + 64], a[:, 256:384],
                                    start=False, stop=True)
                ins.then_inc(s["sb_o"], 1)

            def head_sum(n):
                pe.wait_ge(s["evac"], (MK + n if n < 4 else XQ + n - 4) + 1)
                if n >= 1:
                    pe.wait_ge(s["hn_row"], n)
                for j in range(2):
                    ins = pe.matmul(gps[:, 3, 0:T], ones, sqh[:, n % 2, j * T:(j + 1) * T],
                                    start=(j == 0), stop=(j == 1))
                ins.then_inc(s["hn_sum"], 1)

            def cx_scores(h):
                pe.wait_ge(s["hn_norm"], 4 + h + 1)
                if h >= 2:
                    pe.wait_ge(s["cx_exp"], 2 * (h - 1))
                for t in range(2):
                    for j in range(2):
                        ins = pe.matmul(aps[:, h % 2, t * T:(t + 1) * T],
                                        qx[:, 2 * h + j, t * P:(t + 1) * P], kx[:, 2 * h + j, :],
                                        start=(j == 0), stop=(j == 1))
                ins.then_inc(s["cx_s"], 1)

            def cx_transpose(h):
                pe.wait_ge(s["cx_p"], h + 1)
                if h >= 1:
                    pe.wait_ge(s["cx_pt"], h)
                for m in range(2):
                    for t in range(2):
                        ins = pe.transpose(aps[:, 3, m * T + t * P:m * T + (t + 1) * P],
                                           xp[:, t, m * P:(m + 1) * P], ident)
                ins.then_inc(s["cx_t"], 1)

            def cx_values(h):
                pe.wait_ge(s["cx_pt"], h + 1)
                if h >= 1:
                    pe.wait_ge(s["cx_oe"], h)
                for j in range(2):
                    for m in range(2):
                        c = h * 256 + j * P
                        ins = pe.matmul(aps[:, 2, j * T:(j + 1) * T], vx[:, m, c:c + P],
                                        xpt[:, m * T:(m + 1) * T], start=(m == 0), stop=(m == 1))
                ins.then_inc(s["cx_o"], 1)

            pe.wait_ge(s["par_loaded"], 32)
            column_sums(B5, aps[:, 3, 0:T], (s["nsq"], 0), s["nsum"])
            for h in range(FFN1):
                if h >= 3:
                    pe.wait_ge(s["evac"], h - 2)
                if h < SV:
                    rows_first(0, h, h % 3, H_hi, H_lo, (s["nlo"], 0) if h == 0 else None)
                elif h < CC:
                    tokens_first(0, h, h % 3, H_hi, H_lo)
                elif h < MK or XQ <= h < XQ + 4:
                    rows_first(0, h, h % 3, H_hi, H_lo)
                elif h < MV:
                    rows_first(0, h, h % 3, R_hi, R_lo, (s["nlo"], 4) if h == MK else None)
                elif h < XQ:
                    tokens_first(0, h, h % 3, R_hi, R_lo)
                elif h < WO1:
                    if (h - 36) % 2 == 0:
                        rows_first(0, h, h % 3, H_hi, H_lo)
                    elif h < GATED["x"]:
                        if h == GATED["sb"] + 1:
                            pe.wait_ge(s["sb_olo"], SB_PAIRS)
                        rows_first(0, h, h % 3, Q_hi, Q_lo)
                    elif h < GATED["conv"]:
                        rows_first(0, h, h % 3, Q_hi, Q_lo, (s["ox_lo"], 0) if h == GATED["x"] + 1 else None)
                    else:
                        if h == GATED["conv"] + 1:
                            pe.wait_ge(s["cv_lo"], 4)
                        rows_first(0, h, h % 3, R_hi, R_lo)
                else:
                    rows_first(0, h, h % 3, Q_hi, Q_lo, (s["mg_lo"], 0) if h == WO1 else None)
                if h == 1:
                    pe.wait_ge(s["nrow"], 1)
                    column_sums(B5, aps[:, 3, 0:T], (s["nsq"], 2), s["nsum"])
                if h >= 12 and h % 2 == 0 and h <= 30:
                    t = (h - 12) // 2
                    if t >= 2:
                        sb_values(t - 2)
                    if t < SB_PAIRS:
                        if t == 0:
                            pe.wait_ge(s["evac"], CC)
                            pe.wait_ge(s["nrow"], 2)
                        sb_scores(t)
                    if 1 <= t <= SB_PAIRS:
                        sb_between(t - 1)
                if MK + 1 <= h <= MK + 4 or XQ + 1 <= h <= XQ + 4:
                    head_sum(h - MK - 1 if h < XQ else 4 + h - XQ - 1)
                x0 = XQ + 3
                if x0 + 2 <= h < x0 + 2 + X_HEADS:
                    cx_values(h - x0 - 2)
                if x0 + 1 <= h < x0 + 1 + X_HEADS:
                    cx_transpose(h - x0 - 1)
                if x0 + 1 == h:
                    pass
                if x0 <= h < x0 + X_HEADS:
                    if h > x0:
                        cx_scores(h - x0)
                    else:
                        cx_scores(0)
            column_sums(B5, aps[:, 3, 0:T], (s["nsq"], 4), s["nsum"])
            pe.wait_ge(s["evac"], EVACS1)
            pe.wait_ge(s["nrow"], 3)
            ffn(0, FFN1, 0, None, (s["nlo"], 8))

            pe.wait_ge(s["con_loaded"], 16)
            with pe.Fori(0, LAYERS) as ly:
                h0 = ly * HALVES2 + HALVES1
                e0 = ly * EVACS2 + EVACS1
                f0 = ly * 8

                def fox_scores(h):
                    pe.wait_ge(s["f_m"], f0 + (h + 1))
                    if h >= 2:
                        pe.wait_ge(s["fx_l"], f0 + (h - 1))
                    q = fq[64 * (h % 2):64 * (h % 2) + 64, h // 2, :]
                    k = fk[64 * (h % 2):64 * (h % 2) + 64, h // 2, :]
                    m = fm[:, h % 2, :]
                    o = aps[:, h % 2, :]
                    pe.matmul(o[:, 0:128], q[:, 0:128], k[:, 0:128], start=True, stop=False)
                    pe.matmul(o[:, 0:128], m[:, 0:128], gt, start=False, stop=True)
                    pe.matmul(o[:, 128:384], q[:, 128:256], k, start=True, stop=False)
                    pe.matmul(o[:, 128:256], m[:, 128:256], gt, start=False, stop=False)
                    pe.matmul(o[:, 128:256], m[:, 256:384], ones, start=False, stop=False)
                    pe.matmul(o[:, 256:384], m[:, 256:384], gt, start=False, stop=True)\
                      .then_inc(s["fx_s"], 1)

                def fox_transpose(h):
                    pe.wait_ge(s["fx_p"], f0 + (h + 1))
                    if h >= 1:
                        pe.wait_ge(s["fx_pt"], f0 + h)
                    for c in range(3):
                        ins = pe.transpose(aps[:, 2, c * P:(c + 1) * P],
                                           fl[:, h % 2, c * P:(c + 1) * P], ident)
                    ins.then_inc(s["fx_t"], 1)

                def fox_values(h):
                    pe.wait_ge(s["fx_pt"], f0 + (h + 1))
                    if h % 2 == 0 and h >= 2:
                        pe.wait_ge(s["fx_oe"], ly * 4 + h // 2)
                    o = aps[64 * (h % 2):64 * (h % 2) + 64, 3, :]
                    pt = fpt[:, h % 2, :]
                    pe.matmul(o[:, 0:256], fv[:, 0, 64 * h:64 * h + 64], pt[:, 0:256],
                              start=True, stop=False)
                    pe.matmul(o[:, 128:256], fv[:, 1, 64 * h:64 * h + 64], pt[:, 256:384],
                              start=False, stop=True).then_inc(s["fx_o"], 1)

                def rotate(r):
                    x = (rq if r < 2 else rk)[:, 2 * (r % 2):2 * (r % 2) + 2, :]
                    if r >= 1:
                        pe.wait_ge(s["rt_x"], ly * 4 + r)
                    pe.wait_ge(s["evac"], e0 + ((LRK if r < 2 else LRV) - 1))
                    pe.matmul(gps[:, 3, :], rot, x, start=True, stop=True).then_inc(s["rt_mm"], 1)

                pe.wait_ge(s["ffn_relu"], ly * 16 + 16)
                pe.wait_ge(s["resid"], ly * 8 + 8)
                for l in range(LFFN):
                    if l >= 4:
                        pe.wait_ge(s["evac"], e0 + (l - 3))
                    elif l >= 2:
                        pe.wait_ge(s["evac"], e0)
                    b = l % 3
                    if l < LFQ:
                        pe.wait_ge(s["lo_ready"], h0 + (l + 1))
                        r = ring(l)
                        for k in range(4):
                            kk = 4 * l + k
                            if k % 2 == 0:
                                pe.wait_ge(s["nlo"], ly * 8 + (12 + kk // 2 + 1))
                            for m in range(2):
                                o = gps[:, 1, m * 8:m * 8 + 8]
                                wh, wl = w_hi[:, r, k * 8:k * 8 + 8], w_lo[:, r, k * 8:k * 8 + 8]
                                xh = H_hi[:, kk, m * P:(m + 1) * P]
                                xl = H_lo[:, kk, m * P:(m + 1) * P]
                                pe.matmul(o, xh, wh, start=(kk == 0 and m == 0), stop=False,
                                          skip_group_check=True)
                                pe.matmul(o, xh, wl, start=False, stop=False, skip_group_check=True)
                                ins = pe.matmul(o, xl, wh, start=False,
                                                stop=(kk == KT - 1 and m == 1), skip_group_check=True)
                        ins.then_inc(s["gemm_done"], 1)
                    elif l < LFV or LRQ <= l < LRV or LRG <= l < LWO:
                        rows_first(h0, l, b, H_hi, H_lo)
                    elif l < LRG:
                        tokens_first(h0, l, b, H_hi, H_lo)
                    else:
                        if l == LWO:
                            pe.wait_ge(s["fx_oe"], ly * 4 + 4)
                            pe.wait_ge(s["gn_lo"], ly * 2 + 2)
                        rows_first(h0, l, b, Q_hi, Q_lo)
                    if 7 <= l < 15:
                        if l == 7:
                            pe.wait_ge(s["evac"], e0 + (LRQ - 1))
                        fox_values(l - 7)
                    if 6 <= l < 14:
                        fox_transpose(l - 6)
                    if 5 <= l < 13:
                        if l == 5:
                            pe.wait_ge(s["evac"], e0 + (LFV - 1))
                        fox_scores(l - 5)
                    if 10 <= l < 14:
                        rotate(l - 10)
                    if l == LRG:
                        pe.wait_ge(s["rt_x"], ly * 4 + 4)
                        pe.wait_ge(s["fx_l"], f0 + 8)
                        pe.wait_ge(s["fx_pt"], f0 + 8)
                        for h in range(RET_HEADS):
                            sc = aps[:, h, :] if h < 3 else gps[:, 3, :]
                            pe.matmul(sc[:, 0:256], rk[:, h, 0:128], rq[:, h, :], start=True, stop=True)
                            pe.matmul(sc[:, 256:384], rk[:, h, 128:256], rq[:, h, 128:256],
                                      start=True, stop=True).then_inc(s["rn_s"], 1)
                    if l == LRG + 1:
                        pe.wait_ge(s["rn_m"], ly * 4 + 4)
                        for b2 in range(2):
                            for h in (2 * b2, 2 * b2 + 1):
                                o = aps[:, b2, (h % 2) * T:(h % 2 + 1) * T]
                                pe.matmul(o, rv[:, 0, h * P:(h + 1) * P], inner[:, h, 0:256],
                                          start=True, stop=False)
                                ins = pe.matmul(o[:, 128:256], rv[:, 1, h * P:(h + 1) * P],
                                                inner[:, h, 256:384], start=False, stop=True)
                            ins.then_inc(s["rn_o"], 1)
                        pe.wait_ge(s["fx_oe"], ly * 4 + 4)
                        for b2 in range(2):
                            pe.wait_ge(s["rn_oe"], ly * 2 + (b2 + 1))
                            pe.matmul(aps[:, 2 + b2, :], ones, ro[:, 2 * b2:2 * b2 + 2, :],
                                      start=True, stop=True).then_inc(s["gn_mean"], 1)
                        for b2 in range(2):
                            pe.wait_ge(s["gn_sq"], ly * 2 + (b2 + 1))
                            pe.matmul(aps[:, b2, :], ones, gsq[:, 2 * b2:2 * b2 + 2, :],
                                      start=True, stop=True).then_inc(s["gn_var"], 1)
                pe.wait_ge(s["resid"], ly * 8 + 12)
                column_sums(X, aps[:, 2, 0:T], None, s["nmean"])
                column_sums(B5, aps[:, 3, 0:T], (s["nsq"], ly * 4 + 6), s["nsum"])
                pe.wait_ge(s["evac"], e0 + EVACS2)
                pe.wait_ge(s["nrow"], ly * 2 + 4)
                ffn(h0, LFFN, ly * 16 + 16, None, (s["nlo"], ly * 8 + 16))
                pe.wait_ge(s["resid"], ly * 8 + 16)
                column_sums(X, aps[:, 2, 0:T], None, s["nmean"])
                column_sums(B5, aps[:, 3, 0:T], (s["nsq"], ly * 4 + 8), s["nsum"])


def shape_constants():
    i = np.arange(P)
    c1 = np.zeros((P, CONSTS1), np.float32)
    c1[:, C_ID:C_ID + P] = np.eye(P)
    c1[:, C_GT:C_GT + P] = i[:, None] > i[None, :]
    c1[:, C_LE:C_LE + P] = i[:, None] <= i[None, :]
    c1[:, C_ONE:C_ONE + P] = 1.0
    c1[:, C_PAST:C_PAST + P] = i[:, None] < i[None, :]
    c1[:, C_EPS], c1[:, C_EPS + 1] = EPS_RMS, EPS_LN
    c2 = np.zeros((P, CONSTS2), np.float32)
    half = P // 2
    inv = np.float32(10000.0) ** (-np.arange(half, dtype=np.float32) / np.float32(half))
    ang = np.arange(T, dtype=np.float32)[None, :] * inv[:, None]
    c2[:, C_COS:C_COS + T] = np.tile(np.cos(ang), (2, 1))
    c2[:, C_SIN:C_SIN + T] = np.tile(np.sin(ang), (2, 1))
    log_g = np.log(1.0 - 2.0 ** (-5.0 - np.arange(RET_HEADS)))
    diff = np.arange(T)[None, :] - i[:, None]
    for h in range(RET_HEADS):
        c2[:, C_DECAY + h * T:C_DECAY + (h + 1) * T] = np.where(
            diff >= 0, np.exp(log_g[h] * np.maximum(diff, 0)), 0.0)
    for d in range(half):
        c2[d + half, C_ROT + d] = -1.0
        c2[d, C_ROT + d + half] = 1.0
    block = np.where(i[None, :] <= i[:, None], 0.0, -3.0e38)
    c2[:, C_CAUSAL:C_CAUSAL + P] = block
    c2[:, C_CAUSAL + 2 * P:C_CAUSAL + 3 * P] = block
    return c1, c2


def kernel(**inputs):
    import concourse.bacc as bacc
    from concourse.bass_utils import run_bass_kernel_spmd as run

    a = {k: np.ascontiguousarray(v) for k, v in inputs.items()}

    def halves(w):
        j = w.shape[1] // 256
        return w.reshape(KT, P, j, 256).transpose(2, 1, 0, 3).reshape(j, P, HALF)

    def down_halves(w):
        return w.reshape(8, 4, P, 2, 512).transpose(0, 3, 2, 1, 4).reshape(16, P, HALF)

    def mlp_order(up, down):
        u, d = halves(up), down_halves(down)
        parts = [u[0:2], u[2:4], d[0:2]]
        for j in range(2, 8):
            parts += [u[2 * j:2 * j + 2], d[2 * j - 2:2 * j]]
        return parts + [d[14:16]]

    def pairs(g, w):
        return [x[i:i + 1] for i in range(4) for x in (g, w)]

    win, kv = a["w_in"][0], a["w_mem_kv"][0]
    col = [halves(win[:, i * D:(i + 1) * D]) for i in range(10)]
    c_h, c_b, c_c, sq, sk, sv, xq, g0, g1, g2 = col
    w1 = np.concatenate(
        [sq, sk, sv, c_c, c_h, c_b, halves(kv[:, :D]), halves(kv[:, D:]), xq]
        + pairs(g1, halves(a["w_sb_out"][0])) + pairs(g2, halves(a["w_x_out"][0]))
        + pairs(g0, halves(a["w_conv_out"][0])) + [halves(a["w_out"][0])]
        + mlp_order(a["w_up"][0], a["w_down"][0]))
    w2, wf = [], []
    for ly in range(LAYERS):
        w = a["w_in_2"][ly]
        w2.append(np.concatenate(
            [halves(w[:, :1536]), halves(w[:, 1544:]), halves(a["w_out_2"][ly])]
            + mlp_order(a["w_ff1_2"][ly], a["w_ff2_2"][ly])))
        wf.append(w[:, 1536:1544].reshape(2, 4, P, 8).transpose(0, 2, 1, 3).reshape(2, P, 32))

    def cols(v):
        return v.reshape(-1, P).T

    par1 = np.concatenate([cols(a[n]) for n in ("g_mix", "g_mem", "g_mlp", "q_norm_g", "k_norm_g")]
                          + [cols(a["conv_w"][0, j]) for j in range(3)], axis=1)
    par2 = np.stack([np.concatenate(
        [cols(a[n][ly]) for n in ("ln1_g_2", "ln1_b_2", "ln2_g_2", "ln2_b_2", "ret_gn_g_2")]
        + [np.broadcast_to(a["b_forget_2"][ly], (P, FOX_HEADS))], axis=1) for ly in range(LAYERS)])
    con1, con2 = shape_constants()
    arrays = {"mem_t": a["mem"][0].T, "x_t": a["x"][0].T, "w1": w1, "w2": np.stack(w2),
              "wf": np.stack(wf), "par1": par1, "par2": par2, "con1": con1, "con2": con2}
    arrays = {k: np.ascontiguousarray(v) for k, v in arrays.items()}
    nc = bacc.Bacc("TRN2", target_bir_lowering=False, num_devices=1)
    args = [nc.dram_tensor(k, v.shape, mybir.dt.from_np(v.dtype), kind="ExternalInput").ap()
            for k, v in arrays.items()]
    out = nc.dram_tensor("out_t", (D, T), F32, kind="ExternalOutput").ap()
    build(nc, *args, out)
    r = run(nc, [arrays], core_ids=[0])
    return np.ascontiguousarray(r.results[0]["out_t"].T).reshape(1, T, D)
```

```python
import numpy as np
import concourse.bass as bass
from concourse import mybir
from contextlib import ExitStack


F32 = mybir.dt.float32
F32R = mybir.dt.float32r
ALU = mybir.AluOpType
ACT = mybir.ActivationFunctionType
AX = mybir.AxisListType

P = 128
D = 1024
T = 256
KT = D // P
FF = 4 * D
HALF = KT * 256
LAYERS = 2
EPS_RMS, EPS_LN, EPS_GN = 1e-6, 1e-5, 1e-5
ALPHA = (2 * LAYERS) ** 0.25

SQ, SK, SV, CC, CH, CB, MK, MV, XQ = range(0, 36, 4)
GATED = {"sb": 36, "x": 44, "conv": 52}
WO1 = 60
MEM0 = 4
SB0 = 10
HN0 = 29
FFN1 = 64
HALVES1 = 96
LFQ, LF, LFK, LFV, LRQ, LRK, LRV, LRG, LWO, LFFN = 0, 2, 4, 6, 8, 10, 12, 14, 16, 20
HALVES2 = 52
EVACS1, EVACS2 = 60, 15
FOX_HEADS, RET_HEADS = 8, 4
SB_PAIRS, X_HEADS = 8, 4

G_MIX, G_MEM, G_MLP, G_Q, G_K, CONVW = 0, 8, 16, 24, 26, 28
PARAMS1 = 52
LN1_G, LN1_B, LN2_G, LN2_B, GN_G, B_F = 0, 8, 16, 24, 32, 36
PARAMS2 = 44
C_ID, C_GT, C_LE, C_ONE, C_PAST, CONSTS1 = 0, 128, 256, 384, 512, 640
C_COS, C_SIN, C_DECAY, C_ROT, C_CAUSAL, CONSTS2 = 0, 256, 512, 1536, 1664, 2048

ACT_STEPS_LAYER = 6
DVE_STEPS_LAYER = 51


class Steps:

    def __init__(self, eng, sem, base=0):
        self.eng, self.sem, self.base, self.n = eng, sem, base, 0

    def mark(self, ins):
        ins.then_inc(self.sem, 1)
        self.n += 1

    def settle(self):
        self.eng.wait_ge(self.sem, self.base + self.n)


def build(nc, mem_t, x_t, w1, w2, wf, par1, par2, con1, con2, out_t):
    with ExitStack() as ctx:
        def sb(name, shape, dt=F32):
            return ctx.enter_context(nc.sbuf_tensor(name, shape, dt))

        def sem(name):
            return ctx.enter_context(nc.semaphore(name))

        raw = sb("raw", [P, 2, HALF])
        w_hi = sb("w_hi", [P, 4, HALF], F32R)
        w_lo = sb("w_lo", [P, 4, HALF], F32R)
        H_hi, H_lo = sb("H_hi", [P, KT, T], F32R), sb("H_lo", [P, KT, T], F32R)
        R_hi, R_lo = sb("R_hi", [P, KT, T], F32R), sb("R_lo", [P, KT, T], F32R)
        Q_hi, Q_lo = sb("Q_hi", [P, KT, T], F32R), sb("Q_lo", [P, KT, T], F32R)
        B1, B2, B3 = (sb(f"B{i}", [P, KT, T]) for i in (1, 2, 3))
        B4 = sb("B4", [P, KT, T + 2])
        B5, B6, B7 = (sb(f"B{i}", [P, KT, T]) for i in (5, 6, 7))
        spb = sb("spb", [P, 2, 2, 384])
        soft = sb("soft", [P, 2, 384])
        staged = sb("staged", [P, 2, 512])
        sqh = sb("sqh", [P, 2, 512])
        rs = sb("rs", [P, 3, T])
        cst = sb("cst", [P, CONSTS1])
        par = sb("par", [P, PARAMS1])
        lpar = sb("lpar", [P, PARAMS2])
        small = sb("small", [P, 4, 16])
        fgate = sb("fgate", [P, 2, 16])

        ident, gt = cst[:, C_ID:C_ID + P], cst[:, C_GT:C_GT + P]
        le_one = cst[:, C_LE:C_LE + 2 * P]
        le, ones = cst[:, C_LE:C_LE + P], cst[:, C_ONE:C_ONE + P]
        past = cst[:, C_PAST:C_PAST + P]
        one_col = cst[:, C_ONE:C_ONE + 1]

        qs, ks = B1, B2
        vs = B3[:, :, :].rearrange("p a t -> p (a t)").rearrange("p (m n) -> p m n", m=2)
        u, y = B4, B5
        kx, qx = B6, B7
        vx = B4[:, :, :].rearrange("p a t -> p (a t)")[:, 0:2 * D].rearrange("p (m n) -> p m n", m=2)
        merged, ox = B1, B3
        b5 = B5[:, :, :].rearrange("p a t -> p (a t)")
        xp, xpt = b5[:, 0:512].rearrange("p (m n) -> p m n", m=2), b5[:, 512:1024]
        gate = b5[:, 1024:2048].rearrange("p (m n) -> p m n", m=2)
        X = B2
        hid_s = spb[:, :, :, :].rearrange("p a b t -> p (a b t)")[:, 0:1024].rearrange(
            "p (a n) -> p a n", a=2)
        fq, fk = B1[:, 0:4, :], B1[:, 4:8, :]
        b3 = B3[:, :, :].rearrange("p a t -> p (a t)")
        fv = b3[:, 0:1024].rearrange("p (m n) -> p m n", m=2)
        rv = b3[:, 1024:2048].rearrange("p (m n) -> p m n", m=2)
        b4 = B4[:, :, :].rearrange("p a t -> p (a t)")
        inner = b4[:, 0:1536].rearrange("p (h n) -> p h n", h=4)
        rott = b4[:, 1536:2048].rearrange("p (h n) -> p h n", h=2)
        rq, rk = B5[:, 0:4, :], B5[:, 4:8, :]
        rg, ro = B6[:, 0:4, :], B6[:, 4:8, :]
        gsq, gr0 = B1[:, 0:4, :], B1[:, 4:8, :]
        gv, ga = B5[:, 0:4, :], B5[:, 4:8, :]
        rsig = sqh[:, :, :].rearrange("p a n -> p (a n)").rearrange("p (h n) -> p h n", h=4)
        con = B7[:, :, :].rearrange("p a t -> p (a t)")
        cos_b = con[:, C_COS:C_COS + T].unsqueeze(1).to_broadcast([P, 2, T])
        sin_b = con[:, C_SIN:C_SIN + T].unsqueeze(1).to_broadcast([P, 2, T])
        decay = con[:, C_DECAY:C_DECAY + 4 * T].rearrange("p (h n) -> p h n", h=4)
        rot = con[:, C_ROT:C_ROT + P]
        causal = con[:, C_CAUSAL:C_CAUSAL + 384]
        fm = soft
        gate_rows = soft[0:FOX_HEADS, 0, 0:T]
        fl = spb[:, 0, :, :]
        fpt = spb[:, 1, :, :]

        gps = ctx.enter_context(nc.psum_tensor("gps", [P, 4, 512], F32))
        aps = ctx.enter_context(nc.psum_tensor("aps", [P, 4, 512], F32))

        raw_loaded = [sem("raw_loaded0"), sem("raw_loaded1")]
        names = """in_loaded0 in_loaded1 mem_loaded x_loaded par_loaded con_loaded lpar_loaded out_stored
            hi_ready lo_ready gemm_done evac act_step dve_step act_step2 dve_step2 pads
            nsq nsum nvar nlog nrow nt nhi nlo nres resid acc_ready sqsum
            lpre lmean lcent lsq lpsq lshift lsum
            staged_free conv_y cv_hi cv_lo
            sb_z sb_sp sb_soft sb_lb sb_t sb_arg sb_e sb_a sb_o sb_ohi sb_olo
            hsq hn_sum hn_var hn_log hn_row hn_norm
            cx_s cx_max cx_exp cx_p cx_t cx_pt cx_o cx_oe ox_hi ox_lo
            mg mg_hi mg_lo ffn_relu ffn_sq ffn_hi hidden
            f_cols f_gate f_logit f_sp f_m fx_s fx_l fx_max fx_e fx_p fx_t fx_pt fx_o fx_ohi fx_oe
            rt_mm rt_x rn_s rn_m rn_o rn_oe gn_mean gn_c gn_sq gn_var gn_v gn_log gn_y gn_hi gn_lo""".split()
        s = {n: sem(n) for n in names}
        block = ctx.enter_context(nc.Block())

        def raw_slot(l):
            return l % 2

        def ring(l):
            return l % 4

        def retention_bank(h):
            return (aps[:, 0, :], aps[:, 1, :], gps[:, 3, :], aps[:, 2, :])[h]

        def raw_count(h0, l):
            return h0 * 8 + (l // 2 + 1) * 16

        @block.sync
        def _(sp):
            def load(h0, l, src, first=False, n=HALF):
                if not first:
                    sp.wait_ge(s["lo_ready"], h0 + (l - 1))
                sp.dma_start(raw[:, raw_slot(l), 0:n], src).then_inc(raw_loaded[raw_slot(l)], 16)

            for a in range(2):
                sp.dma_start(B6[:, 4 * a:4 * a + 4, :],
                             x_t[a * D // 2:(a + 1) * D // 2].rearrange("(k p) t -> p k t", p=P))\
                  .then_inc(s[f"in_loaded{a}"], 16)
            sp.dma_start(par[:, :], par1).then_inc(s["par_loaded"], 16)
            sp.dma_start(cst[:, :], con1).then_inc(s["par_loaded"], 16)
            load(0, 0, w1[0], first=True)
            load(0, 1, w1[1], first=True)
            load(0, 2, w1[2])
            load(0, 3, w1[3])
            sp.dma_start(B7[:, :, :], mem_t.rearrange("(k p) t -> p k t", p=P)).then_inc(s["mem_loaded"], 16)
            with sp.Fori(0, 17) as i:
                for a in range(2):
                    sp.wait_ge(s["lo_ready"], i * 2 + a + 3)
                    sp.dma_start(raw[:, a, :], w1[i * 2 + a + 4]).then_inc(raw_loaded[a], 16)
            sp.wait_ge(s["sb_z"], SB_PAIRS)
            sp.dma_start(X[:, :, :], x_t.rearrange("(k p) t -> p k t", p=P)).then_inc(s["x_loaded"], 16)
            with sp.Fori(0, (HALVES1 - 38) // 2) as i:
                for a in range(2):
                    sp.wait_ge(s["lo_ready"], i * 2 + a + 37)
                    sp.dma_start(raw[:, a, :], w1[i * 2 + a + 38]).then_inc(raw_loaded[a], 16)
            sp.wait_ge(s["cx_s"], X_HEADS)
            sp.dma_start(con, con2).then_inc(s["con_loaded"], 16)
            for a in range(2):
                load(HALVES1, a, w2[a])
            for a in range(2):
                load(HALVES1, LF + a, wf[0, a], n=32)
            with sp.Fori(0, LAYERS) as ly:
                h0 = ly * HALVES2 + HALVES1
                def load_pair(i):
                    for a in range(2):
                        sp.wait_ge(s["lo_ready"], h0 + i * 2 + (a + 3))
                        sp.dma_start(raw[:, a, :], w2[ly * (HALVES2 - 2) + i * 2 + (a + 2)])\
                          .then_inc(raw_loaded[a], 16)

                load_pair(0)
                sp.wait_ge(s["nlo"], ly * 8 + 16)
                sp.dma_start(lpar[:, :], par2[ly]).then_inc(s["lpar_loaded"], 16)
                with sp.Fori(1, (HALVES2 - 2) // 2) as i:
                    load_pair(i)
                for a in range(2):
                    load(h0, HALVES2 + LF + a, wf[ly + 1, a], n=32)
            sp.wait_ge(s["nres"], 4 * 2 * LAYERS)
            sp.dma_start(out_t.rearrange("(k p) t -> p k t", p=P), X[:, :, :]).then_inc(s["out_stored"], 16)
            sp.wait_ge(s["out_stored"], 16)

        @block.scalar
        def _(act):
            st = Steps(act, s["act_step"])

            def split(h0, l, n=HALF, start=False):
                act.wait_ge(raw_loaded[raw_slot(l)], raw_count(h0, l))
                if not start:
                    act.wait_ge(s["gemm_done"], h0 + (l - 3))
                act.activation(w_hi[:, ring(l), 0:n], raw[:, raw_slot(l), 0:n], ACT.Copy)\
                   .then_inc(s["hi_ready"], 1)

            def split_gates(h0, l0):
                for a in range(2):
                    split(h0, l0 + LF + a, n=32)

            def bank(l, ringsize=3):
                return gps[:, l % ringsize, :]

            def two(ap):
                return ap.rearrange("p (a t) -> p a t", a=2)

            def evac(dst, src, done, scale=1.0):
                act.wait_ge(s["gemm_done"], done)
                act.activation(dst, src, ACT.Copy, scale=scale).then_inc(s["evac"], 1)

            def rsqrt_start(v, tmp, r0, done):
                st.mark(act.activation(tmp, v, ACT.Ln))
                st.settle()
                act.activation(r0, tmp, ACT.Exp, scale=-0.5).then_inc(done, 1)

            def squares(src, sq, q0, q1, done):
                act.activation(sq[:, 2 * q0:2 * q1, 0:T], src[:, 2 * q0:2 * q1, :], ACT.Square)\
                   .then_inc(done, 1)

            def rms_norm(i, nbuf, hi):
                act.wait_ge(s["nvar"], i + 1)
                rsqrt_start(rs[:, 2, :], rs[:, 0, :], rs[:, 1, :], s["nlog"])
                for q in range(4):
                    act.wait_ge(s["nt"], i * 4 + (q + 1))
                    act.activation(hi[:, 2 * q:2 * q + 2, :], nbuf[:, 2 * q:2 * q + 2, 0:T], ACT.Copy)\
                       .then_inc(s["nhi"], 1)

            def layer_norm(n, r0, hi, g, b, after_squares=None):
                act.wait_ge(s["resid"], r0 + 3)
                squares(X, B5, 2, 3, s["lsq"])
                act.wait_ge(s["lcent"], n + 1)
                squares(X, B5, 0, 2, s["lsq"])
                act.wait_ge(s["resid"], r0 + 4)
                squares(X, B5, 3, 4, s["lsq"])
                if after_squares is not None:
                    after_squares()
                act.wait_ge(s["nvar"], n + 4)
                rsqrt_start(rs[:, 2, :], rs[:, 0, :], rs[:, 0, :], s["nlog"])
                for q in range(4):
                    act.wait_ge(s["nt"], n * 4 + (12 + q + 1))
                    for k in (2 * q, 2 * q + 1):
                        ins = act.activation(X[:, k, :], B1[:, k, :], ACT.Identity,
                                             bias=lpar[:, b + k:b + k + 1],
                                             scale=lpar[:, g + k:g + k + 1])
                    ins.then_inc(s["nres"], 1)
                    act.wait_ge(s["nres"], n * 4 + (q + 1))
                    act.activation(hi[:, 2 * q:2 * q + 2, :], X[:, 2 * q:2 * q + 2, :], ACT.Copy)\
                       .then_inc(s["nhi"], 1)

            def up(h, l, uu, par_, a, fresh=False):
                act.wait_ge(s["gemm_done"], h + (l + 1))
                if not fresh:
                    act.wait_ge(s["ffn_sq"], uu - 1)
                act.activation(staged[:, a, :], gps[:, 2 * par_ + a, :], ACT.Relu)\
                   .then_inc(s["ffn_relu"], 1)
                act.wait_ge(s["ffn_relu"], uu + 1)
                t0 = 4 * par_ + 2 * a
                act.activation(Q_hi[:, t0:t0 + 2, :], two(staged[:, a, :]), ACT.Square)\
                   .then_inc(s["ffn_hi"], 1)

            def ffn(h0, l0, ub, first=False):
                split(h0, l0 + 2)
                split(h0, l0 + 3)
                for a in range(2):
                    up(h0, l0 + a, ub + a, 0, a, fresh=first)
                    split(h0, l0 + 4 + a)
                with act.Fori(0, 3) as f:
                    hf, uf = h0 + f * 8, ub + f * 4
                    for a in range(2):
                        up(hf, l0 + 2 + a, uf + (2 + a), 1, a)
                        split(hf, l0 + 6 + a)
                    split(hf, l0 + 8)
                    split(hf, l0 + 9)
                    for a in range(2):
                        up(hf, l0 + 6 + a, uf + (4 + a), 0, a)
                        split(hf, l0 + 10 + a)
                    split(hf, l0 + 12)
                    split(hf, l0 + 13)
                for a in range(2):
                    up(h0, l0 + 26 + a, ub + (14 + a), 1, a)
                    split(h0, l0 + 30 + a)
                split(h0, l0 + 32)
                split(h0, l0 + 33)

            def sb_out(i):
                act.wait_ge(s["sb_o"], i + 1)
                act.activation(Q_hi[:, i, :], gps[:, 3, 0:T], ACT.Copy).then_inc(s["sb_ohi"], 1)

            def sb_softplus(i):
                act.wait_ge(s["sb_z"], i + 1)
                if i >= 2:
                    act.wait_ge(s["sb_o"], i - 1)
                b = spb[:, i % 2, :, :]
                st.mark(act.activation(b, aps[:, 0:2, 0:384], ACT.Abs))
                st.settle()
                st.mark(act.activation(b, b, ACT.Exp, scale=-1.0))
                st.settle()
                act.activation(b, b, ACT.Ln, bias=one_col).then_inc(s["sb_sp"], 1)

            def sb_exp(i):
                act.wait_ge(s["sb_arg"], i + 1)
                b = spb[:, i % 2, :, :]
                act.activation(b, b, ACT.Exp).then_inc(s["sb_e"], 1)

            def head_squares(n):
                i = n % 4
                act.wait_ge(s["evac"], (MK + n if n < 4 else XQ + n - 4) + 1)
                if n >= 2:
                    act.wait_ge(s["hn_sum"], n - 1)
                act.activation(two(sqh[:, n % 2, :]), (kx if n < 4 else qx)[:, 2 * i:2 * i + 2, :],
                               ACT.Square).then_inc(s["hsq"], 1)

            def head_rsqrt(n):
                act.wait_ge(s["hn_var"], n + 1)
                rsqrt_start(rs[:, 2, :], rs[:, 0, :], rs[:, 1, :], s["hn_log"])

            def cx_out(h):
                act.wait_ge(s["cx_o"], h + 1)
                act.activation(ox[:, 2 * h:2 * h + 2, :], two(aps[:, 2, :]), ACT.Copy)\
                   .then_inc(s["cx_oe"], 1)

            def cx_copy(h):
                act.wait_ge(s["cx_t"], h + 1)
                if h >= 1:
                    act.wait_ge(s["cx_o"], h)
                act.activation(xpt, aps[:, 3, :], ACT.Copy).then_inc(s["cx_pt"], 1)

            def cx_exp(h):
                act.wait_ge(s["cx_max"], h + 1)
                if h >= 1:
                    act.wait_ge(s["cx_t"], h)
                for t in range(2):
                    act.activation(xp[:, t, :], aps[:, h % 2, t * T:(t + 1) * T], ACT.Exp,
                                   bias=small[:, 1, 2 * h + t:2 * h + t + 1], scale=1.0 / 16,
                                   accum_out=small[:, 2, 2 * h + t:2 * h + t + 1]).then_inc(s["cx_exp"], 1)

            act.preload_act_table_set("natural_log_exp_and_others")
            for a in range(2):
                act.wait_ge(s[f"in_loaded{a}"], 16)
                squares(B6, B5, 2 * a, 2 * a + 2, s["nsq"])
            split(0, 0, start=True)
            rms_norm(0, B1, H_hi)
            for l in range(1, 4):
                split(0, l, start=True)
            staged_n = 0
            for h in range(FFN1):
                ps = bank(h)
                if h < SK:
                    i = h - SQ
                    evac(qs[:, 2 * i:2 * i + 2, :], two(ps), h + 1, scale=0.125)
                elif h < SV:
                    i = h - SK
                    evac(ks[:, 2 * i:2 * i + 2, :], two(ps), h + 1)
                elif h < CC:
                    i = h - SV
                    evac(vs[:, :, 256 * i:256 * i + 256], two(ps), h + 1)
                elif h < CH:
                    i = h - CC
                    evac(u[:, 2 * i:2 * i + 2, 2:T + 2], two(ps), h + 1)
                elif h < MK:
                    if staged_n >= 2:
                        act.wait_ge(s["staged_free"], staged_n - 1)
                    evac(staged[:, staged_n % 2, :], ps, h + 1)
                    staged_n += 1
                elif h < MV or XQ <= h < XQ + 4:
                    i = h - (MK if h < MV else XQ)
                    evac((kx if h < MV else qx)[:, 2 * i:2 * i + 2, :], two(ps), h + 1)
                elif h < XQ:
                    i = h - MV
                    evac(vx[:, :, 256 * i:256 * i + 256], two(ps), h + 1)
                elif h < WO1:
                    if (h - 36) % 2 == 0:
                        act.wait_ge(s["gemm_done"], h + 1)
                        act.wait_ge(s["staged_free"], staged_n - 1)
                        act.activation(gate[:, staged_n % 2, :], ps, ACT.Sigmoid).then_inc(s["evac"], 1)
                    else:
                        act.wait_ge(s["staged_free"], staged_n - 1)
                        evac(staged[:, staged_n % 2, :], ps, h + 1)
                        staged_n += 1
                        if h > GATED["conv"]:
                            i = (h - GATED["conv"]) // 2
                            act.wait_ge(s["mg"], i + 1)
                            act.activation(Q_hi[:, 2 * i:2 * i + 2, :], merged[:, 2 * i:2 * i + 2, :],
                                           ACT.Copy).then_inc(s["mg_hi"], 1)
                else:
                    if h == WO1:
                        act.preload_act_table_set("natural_log_exp_and_others")
                    act.wait_ge(s["resid"], h - WO1 + 1)
                    squares(X, B5, h - WO1, h - WO1 + 1, s["nsq"])
                if h == MEM0:
                    act.wait_ge(s["mem_loaded"], 16)
                    for a in range(2):
                        squares(B7, B5, 2 * a, 2 * a + 2, s["nsq"])
                if h == MEM0 + 2:
                    rms_norm(1, B4, R_hi)
                if SB0 <= h <= SB0 + 18 and h % 2 == 0:
                    t = (h - SB0) // 2
                    if t >= 2:
                        sb_out(t - 2)
                    if t < SB_PAIRS:
                        sb_softplus(t)
                    if 1 <= t <= SB_PAIRS:
                        sb_exp(t - 1)
                if h + 4 < FFN1 + 2:
                    split(0, h + 4)
                if HN0 - 1 <= h < HN0 + 7:
                    head_squares(h - HN0 + 1)
                if HN0 <= h < HN0 + 8:
                    head_rsqrt(h - HN0)
                if XQ <= h < XQ + 4:
                    i = h - XQ
                    act.wait_ge(s["gemm_done"], XQ)
                    act.wait_ge(s["conv_y"], i + 1)
                    act.activation(R_hi[:, 2 * i:2 * i + 2, :], y[:, 2 * i:2 * i + 2, :], ACT.Copy)\
                       .then_inc(s["cv_hi"], 1)
                if h == XQ + 3:
                    act.wait_ge(s["cv_lo"], 4)
                x0 = XQ + 3
                if x0 + 2 <= h < x0 + 2 + X_HEADS:
                    cx_out(h - x0 - 2)
                if x0 + 1 <= h < x0 + 1 + X_HEADS:
                    cx_copy(h - x0 - 1)
                if x0 <= h < x0 + X_HEADS:
                    cx_exp(h - x0)
                if h == GATED["x"] - 1:
                    act.wait_ge(s["gemm_done"], h + 1)
                    for i in range(4):
                        act.activation(Q_hi[:, 2 * i:2 * i + 2, :], ox[:, 2 * i:2 * i + 2, :], ACT.Copy)\
                           .then_inc(s["ox_hi"], 1)
            rms_norm(2, B1, R_hi)
            act.wait_ge(s["staged_free"], staged_n)
            ffn(0, FFN1, 0, first=True)
            split_gates(HALVES1, 0)
            for q in range(4):
                act.wait_ge(s["resid"], 4 + q + 1)
                act.activation(H_hi[:, 2 * q:2 * q + 2, :], X[:, 2 * q:2 * q + 2, :], ACT.Copy)\
                   .then_inc(s["nhi"], 1)

            with act.Fori(0, LAYERS) as ly:
                st = Steps(act, s["act_step2"], ly * ACT_STEPS_LAYER)
                h0 = ly * HALVES2 + HALVES1
                e0 = ly * EVACS2 + EVACS1

                def fox_softplus():
                    act.wait_ge(s["f_logit"], ly + 1)
                    fa = small[:, 0, :]
                    st.mark(act.activation(fa, fgate[:, 0, :], ACT.Abs))
                    st.settle()
                    st.mark(act.activation(fa, fa, ACT.Exp, scale=-1.0))
                    st.settle()
                    act.activation(fa, fa, ACT.Ln, bias=one_col).then_inc(s["f_sp"], 1)

                def fox_out(c):
                    act.wait_ge(s["fx_o"], ly * 8 + (2 * c + 2))
                    act.activation(Q_hi[:, c, :], aps[:, 3, 0:T], ACT.Copy).then_inc(s["fx_ohi"], 1)

                def fox_copy(h):
                    act.wait_ge(s["fx_t"], ly * 8 + (h + 1))
                    act.activation(fpt[:, h % 2, :], aps[:, 2, 0:384], ACT.Copy).then_inc(s["fx_pt"], 1)

                def fox_exp(h):
                    act.wait_ge(s["fx_max"], ly * 8 + (h + 1))
                    for t, (c0, c1) in enumerate(((0, 128), (128, 384))):
                        act.activation(fl[:, h % 2, c0:c1], fl[:, h % 2, c0:c1], ACT.Exp,
                                       bias=small[:, 1, 2 * h + t:2 * h + t + 1],
                                       accum_out=small[:, 2, 2 * h + t:2 * h + t + 1])\
                           .then_inc(s["fx_e"], 1)

                act.preload_act_table_set("natural_log_exp_and_others")
                for l in range(LFFN):
                    ps = bank(l)
                    done = h0 + (l + 1)
                    a = l % 2
                    if l == LF:
                        pass
                    elif l == LF + 1:
                        act.wait_ge(s["gemm_done"], done)
                        act.activation(gate_rows, gps[0:FOX_HEADS, LF % 3, 0:T], ACT.Copy)\
                           .then_inc(s["evac"], 1)
                    elif l < LF:
                        evac(fq[:, 2 * a:2 * a + 2, :], two(ps), done, scale=0.125)
                    elif l < LFV:
                        evac(fk[:, 2 * a:2 * a + 2, :], two(ps), done)
                    elif l < LRQ:
                        evac(fv[:, :, 256 * a:256 * a + 256], two(ps), done)
                    elif l < LRK:
                        evac(rq[:, 2 * a:2 * a + 2, :], two(ps), done)
                    elif l < LRV:
                        evac(rk[:, 2 * a:2 * a + 2, :], two(ps), done, scale=P ** -0.5)
                    elif l < LRG:
                        evac(rv[:, :, 256 * a:256 * a + 256], two(ps), done)
                    elif l < LWO:
                        act.wait_ge(s["gemm_done"], done)
                        act.activation(rg[:, 2 * a:2 * a + 2, :], two(ps), ACT.Copy)
                        act.activation(rsig[:, 2 * a:2 * a + 2, :], two(ps), ACT.Sigmoid)\
                           .then_inc(s["evac"], 1)
                    if l == LFK:
                        act.wait_ge(s["f_cols"], ly + 1)
                        act.activation(fgate[:, 0, :], gps[:, 3, 0:16], ACT.Copy).then_inc(s["f_gate"], 1)
                        fox_softplus()
                    if l + 4 < LWO + 3:
                        split(h0, l + 4)
                    if l >= 7 and l <= 14 and l % 2 == 0:
                        fox_out((l - 8) // 2)
                    if 6 <= l < 14:
                        fox_copy(l - 6)
                    if 5 <= l < 13:
                        fox_exp(l - 5)
                    if LRG <= l < LWO:
                        b = l - LRG
                        act.wait_ge(s["rn_o"], ly * 2 + (b + 1))
                        act.activation(ro[:, 2 * b:2 * b + 2, :], two(aps[:, b, :]), ACT.Copy)\
                           .then_inc(s["rn_oe"], 1)
                    if l == LRG + 1:
                        act.preload_act_table_set("natural_log_exp_and_others")
                        for b in range(2):
                            act.wait_ge(s["gn_c"], ly * 2 + (b + 1))
                            act.activation(gsq[:, 2 * b:2 * b + 2, :], ro[:, 2 * b:2 * b + 2, :],
                                           ACT.Square).then_inc(s["gn_sq"], 1)
                        for b in range(2):
                            act.wait_ge(s["gn_v"], ly * 2 + (b + 1))
                            r0 = gr0[:, 2 * b:2 * b + 2, :]
                            rsqrt_start(gv[:, 2 * b:2 * b + 2, :], r0, r0, s["gn_log"])
                        split(h0, LWO + 3)
                        for b in range(2):
                            act.wait_ge(s["gn_y"], ly * 2 + (b + 1))
                            act.activation(Q_hi[:, 4 + 2 * b:6 + 2 * b, :], ro[:, 2 * b:2 * b + 2, :],
                                           ACT.Copy).then_inc(s["gn_hi"], 1)
                        split(h0, LFFN)
                        split(h0, LFFN + 1)
                layer_norm(ly * 2, ly * 8 + 8, R_hi, LN1_G, LN1_B)
                ffn(h0, LFFN, ly * 16 + 16)
                layer_norm(ly * 2 + 1, ly * 8 + 12, H_hi, LN2_G, LN2_B,
                           after_squares=lambda: split_gates(h0, HALVES2))
                assert st.n == ACT_STEPS_LAYER, st.n

        @block.vector
        def _(dve):
            st = Steps(dve, s["dve_step"])

            def split(h0, l, n=HALF):
                dve.wait_ge(s["hi_ready"], h0 + (l + 1))
                dve.tensor_tensor(w_lo[:, ring(l), 0:n], raw[:, raw_slot(l), 0:n],
                                  w_hi[:, ring(l), 0:n].bitcast(F32), ALU.subtract)\
                   .then_inc(s["lo_ready"], 1)

            def two(ap):
                return ap.rearrange("p (a t) -> p a t", a=2)

            def rsqrt(ps, scale, eps, v, r0, a, r, ready, log, count, done, between=None):
                dve.tensor_scalar(v, ps, scale, eps, ALU.mult, ALU.add).then_inc(ready, 1)
                if between is not None:
                    between()
                dve.wait_ge(ready, count)
                dve.wait_ge(log, count)
                newton(v, r0, a, r, done)

            def newton(v, r0, a, r, done):
                st.mark(dve.scalar_tensor_tensor(a, v, -0.5, r0, ALU.mult, ALU.mult))
                st.settle()
                st.mark(dve.tensor_tensor(a, a, r0, ALU.mult))
                st.settle()
                ins = dve.scalar_tensor_tensor(r, a, 1.5, r0, ALU.add, ALU.mult)
                if done is None:
                    st.mark(ins)
                    st.settle()
                else:
                    ins.then_inc(done, 1)

            def normalised(tile, lo_part):
                tile(0)
                tile(1)
                lo_part(0)
                tile(2)
                lo_part(1)
                tile(3)
                lo_part(2)
                lo_part(3)

            def square_sums(squared):
                dve.wait_ge(s["nsq"], squared)
                st.mark(dve.tensor_tensor(B5[:, 0:4, :], B5[:, 0:4, :], B5[:, 4:8, :], ALU.add))
                st.settle()
                dve.tensor_tensor(B5[:, 0:2, :], B5[:, 0:2, :], B5[:, 2:4, :], ALU.add)\
                   .then_inc(s["sqsum"], 1)

            def rms_norm(i, src, nbuf, hi, lo, g, between=None):
                dve.wait_ge(s["nsum"], i + 1)
                rsqrt(aps[:, 3, 0:T], 1.0 / D, EPS_RMS, rs[:, 2, :], rs[:, 1, :], rs[:, 0, :],
                      rs[:, 2, :], s["nvar"], s["nlog"], i + 1, s["nrow"], between)
                dve.wait_ge(s["nrow"], i + 1)

                def tile(q):
                    for k in (2 * q, 2 * q + 1):
                        ins = dve.scalar_tensor_tensor(nbuf[:, k, 0:T], src[:, k, :], g[:, k:k + 1],
                                                       rs[:, 2, :], ALU.mult, ALU.mult)
                    ins.then_inc(s["nt"], 1)

                def lo_part(q):
                    dve.wait_ge(s["nhi"], i * 4 + (q + 1))
                    dve.tensor_tensor(lo[:, 2 * q:2 * q + 2, :], nbuf[:, 2 * q:2 * q + 2, 0:T],
                                      hi[:, 2 * q:2 * q + 2, :].bitcast(F32), ALU.subtract)\
                       .then_inc(s["nlo"], 1)

                normalised(tile, lo_part)

            def rows(r, n):
                return rs[:, r, :].unsqueeze(1).to_broadcast([P, n, T])

            def residual(q, out):
                t = X[:, 2 * q:2 * q + 2, :]
                dve.scalar_tensor_tensor(t, t, ALPHA, out, ALU.mult, ALU.add).then_inc(s["resid"], 1)

            def shifted(q, out):
                t = X[:, 2 * q:2 * q + 2, :]
                dve.tensor_tensor(t, t, out, ALU.add).then_inc(s["resid"], 1)

            def first_half(n, r0):
                dve.wait_ge(s["resid"], r0 + 2)
                dve.tensor_tensor(B1[:, 0:2, :], X[:, 0:2, :], X[:, 2:4, :], ALU.add)\
                   .then_inc(s["lpre"], 1)

            def shift(n):
                dve.wait_ge(s["lmean"], n + 1)
                st.mark(dve.tensor_scalar(rs[:, 1, :], gps[:, 3, 0:T], 2.0 / D, None, ALU.mult))
                st.settle()
                st.mark(dve.scalar_tensor_tensor(X[:, 4:8, :], X[:, 4:8, :], ALPHA, rows(1, 4),
                                                 ALU.mult, ALU.subtract))
                st.settle()

            def shift_first(n):
                dve.tensor_tensor(X[:, 0:4, :], X[:, 0:4, :], rows(1, 4), ALU.subtract)\
                   .then_inc(s["lcent"], 1)

            def early_squares(n):
                dve.wait_ge(s["lsq"], n * 3 + 2)
                dve.tensor_tensor(B5[:, 0:2, :], B5[:, 0:2, :], B5[:, 2:4, :], ALU.add)\
                   .then_inc(s["lpsq"], 1)

            def second_half(n, r0):
                dve.wait_ge(s["resid"], r0 + 4)
                dve.tensor_tensor(B1[:, 0:2, :], X[:, 4:6, :], X[:, 6:8, :], ALU.add)\
                   .then_inc(s["lshift"], 1)

            def layer_norm(n, hi, lo):
                dve.wait_ge(s["lsum"], n + 1)
                st.mark(dve.tensor_scalar(rs[:, 1, :], gps[:, 3, T:2 * T], 1.0 / D, None, ALU.mult))
                st.settle()
                st.mark(dve.scalar_tensor_tensor(rs[:, 0, :], rs[:, 1, :], -1.0, rs[:, 1, :],
                                                 ALU.mult, ALU.mult))
                st.settle()
                st.mark(dve.tensor_scalar(rs[:, 0, :], rs[:, 0, :], EPS_LN, None, ALU.add))
                st.settle()
                dve.wait_ge(s["nsum"], n + 4)
                dve.scalar_tensor_tensor(rs[:, 2, :], aps[:, 0, 0:T], 1.0 / D, rs[:, 0, :],
                                         ALU.mult, ALU.add).then_inc(s["nvar"], 1)
                st.mark(dve.tensor_tensor(X[:, 0:4, :], X[:, 0:4, :], rows(1, 4), ALU.subtract))
                dve.wait_ge(s["nvar"], n + 4)
                dve.wait_ge(s["nlog"], n + 4)
                newton(rs[:, 2, :], rs[:, 0, :], sqh[:, 0, 0:T], rs[:, 2, :], s["nrow"])
                dve.wait_ge(s["nrow"], n + 4)
                st.settle()

                def tile(q):
                    if q == 2:
                        st.mark(dve.tensor_tensor(X[:, 4:8, :], X[:, 4:8, :], rows(1, 4),
                                                  ALU.subtract))
                        st.settle()
                    dve.tensor_tensor(B1[:, 2 * q:2 * q + 2, :], X[:, 2 * q:2 * q + 2, :], rows(2, 2),
                                      ALU.mult).then_inc(s["nt"], 1)

                def lo_part(q):
                    dve.wait_ge(s["nhi"], n * 4 + (16 + q + 1))
                    dve.tensor_tensor(lo[:, 2 * q:2 * q + 2, :], X[:, 2 * q:2 * q + 2, :],
                                      hi[:, 2 * q:2 * q + 2, :].bitcast(F32), ALU.subtract)\
                       .then_inc(s["nlo"], 1)

                normalised(tile, lo_part)

            def up(uu, par_, a):
                t0 = 4 * par_ + 2 * a
                dve.wait_ge(s["ffn_relu"], uu + 1)
                dve.tensor_tensor(hid_s[:, a, :], staged[:, a, :], staged[:, a, :], ALU.mult)\
                   .then_inc(s["ffn_sq"], 1)
                dve.wait_ge(s["ffn_sq"], uu + 1)
                dve.wait_ge(s["ffn_hi"], uu + 1)
                dve.tensor_tensor(Q_lo[:, t0:t0 + 2, :], two(hid_s[:, a, :]),
                                  Q_hi[:, t0:t0 + 2, :].bitcast(F32), ALU.subtract)\
                   .then_inc(s["hidden"], 1)

            def ffn(h0, l0, ub):
                split(h0, l0 + 2)
                split(h0, l0 + 3)
                for a in range(2):
                    up(ub + a, 0, a)
                    split(h0, l0 + 4 + a)
                with dve.Fori(0, 3) as f:
                    hf, uf = h0 + f * 8, ub + f * 4
                    for a in range(2):
                        up(uf + (2 + a), 1, a)
                        split(hf, l0 + 6 + a)
                    split(hf, l0 + 8)
                    split(hf, l0 + 9)
                    for a in range(2):
                        up(uf + (4 + a), 0, a)
                        split(hf, l0 + 10 + a)
                    split(hf, l0 + 12)
                    split(hf, l0 + 13)
                for a in range(2):
                    up(ub + (14 + a), 1, a)
                    split(h0, l0 + 30 + a)
                split(h0, l0 + 32)
                split(h0, l0 + 33)

            diag2 = past.unsqueeze(1).to_broadcast([P, 2, P])

            def mask_diagonals(b, done):
                for hh in range(2):
                    t = b[:, hh, :].rearrange("p (c n) -> p c n", c=3)[:, 0:3:2, :]
                    ins = dve.tensor_tensor(t, t, diag2, ALU.mult)
                ins.then_inc(done, 1)

            def sb_out(i):
                dve.wait_ge(s["sb_ohi"], i + 1)
                dve.tensor_tensor(Q_lo[:, i, :], gps[:, 3, 0:T], Q_hi[:, i, :].bitcast(F32),
                                  ALU.subtract).then_inc(s["sb_olo"], 1)

            def sb_parts(i):
                b, z = spb[:, i % 2, :, :], aps[:, 0:2, 0:384]
                dve.wait_ge(s["sb_sp"], i + 1)
                if i >= 1:
                    dve.wait_ge(s["sb_t"], i)
                st.mark(dve.scalar_tensor_tensor(soft[:, :, :], z, 0.0, b, ALU.max, ALU.add))
                st.settle()
                mask_diagonals(soft, s["sb_soft"])
                dve.scalar_tensor_tensor(b, z, 0.0, b, ALU.min, ALU.subtract).then_inc(s["sb_lb"], 1)

            def sb_arg(i):
                b = spb[:, i % 2, :, :]
                dve.wait_ge(s["sb_t"], i + 1)
                dve.wait_ge(s["sb_lb"], i + 1)
                dve.tensor_tensor(b, b, aps[:, 2:4, 0:384], ALU.subtract).then_inc(s["sb_arg"], 1)

            def sb_mask(i):
                dve.wait_ge(s["sb_e"], i + 1)
                mask_diagonals(spb[:, i % 2, :, :], s["sb_a"])

            def head_norm(n):
                i = n % 4
                dst = kx if n < 4 else qx
                g = G_K if n < 4 else G_Q
                dve.wait_ge(s["hn_sum"], n + 1)
                if n >= 1:
                    dve.wait_ge(s["hn_norm"], n)
                rsqrt(gps[:, 3, 0:T], 1.0 / 256, EPS_RMS, rs[:, 2, :], rs[:, 1, :], rs[:, 0, :],
                      rs[:, 2, :], s["hn_var"], s["hn_log"], n + 1, s["hn_row"])
                dve.wait_ge(s["hn_row"], n + 1)
                for j in range(2):
                    t = dst[:, 2 * i + j, :]
                    ins = dve.scalar_tensor_tensor(t, t, par[:, g + j:g + j + 1], rs[:, 2, :],
                                                   ALU.mult, ALU.mult)
                ins.then_inc(s["hn_norm"], 1)

            def cx_max(h):
                dve.wait_ge(s["cx_s"], h + 1)
                st.mark(dve.tensor_reduce(small[:, 0, 2 * h:2 * h + 2], two(aps[:, h % 2, :]),
                                          AX.X, ALU.max))
                st.settle()
                dve.tensor_scalar(small[:, 1, 2 * h:2 * h + 2], small[:, 0, 2 * h:2 * h + 2],
                                  -1.0 / 16, None, ALU.mult).then_inc(s["cx_max"], 1)

            def cx_scale(h):
                dve.wait_ge(s["cx_exp"], 2 * h + 2)
                st.mark(dve.reciprocal(small[:, 3, 2 * h:2 * h + 2], small[:, 2, 2 * h:2 * h + 2]))
                st.settle()
                for t in range(2):
                    ins = dve.tensor_scalar(xp[:, t, :], xp[:, t, :],
                                            small[:, 3, 2 * h + t:2 * h + t + 1], None, ALU.mult)
                ins.then_inc(s["cx_p"], 1)

            square_sums(2)
            dve.wait_ge(s["par_loaded"], 32)
            rms_norm(0, B6, B1, H_hi, H_lo, par[:, G_MIX:G_MIX + KT], between=lambda: split(0, 0))
            for l in range(1, 4):
                split(0, l)
            staged_n = 0
            for h in range(FFN1):
                if SB0 <= h <= SB0 + 18 and h % 2 == 0:
                    t = (h - SB0) // 2
                    if t >= 2:
                        sb_out(t - 2)
                    if 1 <= t <= SB_PAIRS:
                        sb_arg(t - 1)
                    if t < SB_PAIRS:
                        sb_parts(t)
                    if 1 <= t <= SB_PAIRS:
                        sb_mask(t - 1)
                if CH <= h < MK:
                    dve.wait_ge(s["evac"], h + 1)
                    i = (h - CH) % 4
                    sg = two(staged[:, staged_n % 2, :])
                    staged_n += 1
                    if h < CB:
                        t = u[:, 2 * i:2 * i + 2, 2:T + 2]
                        dve.wait_ge(s["pads"], 1)
                        dve.tensor_tensor(t, t, sg, ALU.mult).then_inc(s["staged_free"], 1)
                        dve.wait_ge(s["staged_free"], staged_n)
                        for tap in (2, 1, 0):
                            for k in (2 * i, 2 * i + 1):
                                wc = par[:, CONVW + 8 * tap + k:CONVW + 8 * tap + k + 1]
                                if tap == 2:
                                    ins = dve.tensor_scalar(y[:, k, :], u[:, k, 2:T + 2], wc, None, ALU.mult)
                                else:
                                    ins = dve.scalar_tensor_tensor(y[:, k, :], u[:, k, tap:T + tap], wc,
                                                                   y[:, k, :], ALU.mult, ALU.add)
                            st.mark(ins)
                            st.settle()
                    else:
                        t = y[:, 2 * i:2 * i + 2, :]
                        dve.tensor_tensor(t, t, sg, ALU.mult).then_inc(s["staged_free"], 1)
                elif 36 <= h < WO1 and (h - 36) % 2 == 1:
                    i = (h - 36) // 2 % 4
                    dve.wait_ge(s["evac"], h + 1)
                    m = merged[:, 2 * i:2 * i + 2, :]
                    sg, gg = staged[:, staged_n % 2, :], gate[:, staged_n % 2, :]
                    staged_n += 1
                    if h < GATED["x"]:
                        dve.tensor_tensor(m, two(sg), two(gg), ALU.mult).then_inc(s["staged_free"], 1)
                    else:
                        st.mark(dve.tensor_tensor(sg, sg, gg, ALU.mult))
                        st.settle()
                        dve.tensor_tensor(m, m, two(sg), ALU.add).then_inc(s["staged_free"], 1)
                    if h > GATED["conv"]:
                        dve.wait_ge(s["staged_free"], staged_n)
                        dve.sem_inc(s["mg"], 1)
                        dve.wait_ge(s["mg_hi"], i + 1)
                        dve.tensor_tensor(Q_lo[:, 2 * i:2 * i + 2, :], m,
                                          Q_hi[:, 2 * i:2 * i + 2, :].bitcast(F32), ALU.subtract)\
                           .then_inc(s["mg_lo"], 1)
                elif h >= WO1:
                    i = h - WO1
                    dve.wait_ge(s["gemm_done"], h + 1)
                    dve.wait_ge(s["x_loaded"], 16)
                    t = X[:, 2 * i:2 * i + 2, :]
                    dve.tensor_tensor(t, t, two(gps[:, h % 3, :]), ALU.add).then_inc(s["resid"], 1)
                    if 1 <= i < 3:
                        dve.wait_ge(s["nsq"], 4 + i + 1)
                        ins = dve.tensor_tensor(B5[:, 0:2, :], B5[:, 0:2, :], B5[:, 2 * i:2 * i + 2, :],
                                                ALU.add)
                        if i == 1:
                            st.mark(ins)
                            st.settle()
                        else:
                            ins.then_inc(s["sqsum"], 1)
                if h == MEM0:
                    square_sums(4)
                if h == MEM0 + 2:
                    rms_norm(1, B7, B4, R_hi, R_lo, par[:, G_MEM:G_MEM + KT])
                    dve.wait_ge(s["nlo"], 8)
                    dve.memset(u[:, :, 0:2], 0.0).then_inc(s["pads"], 1)
                if HN0 <= h < HN0 + 8:
                    head_norm(h - HN0)
                if XQ <= h < XQ + 4:
                    i = h - XQ
                    if i == 0:
                        dve.wait_ge(s["staged_free"], 8)
                        dve.sem_inc(s["conv_y"], 4)
                    dve.wait_ge(s["cv_hi"], i + 1)
                    dve.tensor_tensor(R_lo[:, 2 * i:2 * i + 2, :], y[:, 2 * i:2 * i + 2, :],
                                      R_hi[:, 2 * i:2 * i + 2, :].bitcast(F32), ALU.subtract)\
                       .then_inc(s["cv_lo"], 1)
                x0 = XQ + 3
                if x0 <= h < x0 + X_HEADS:
                    cx_max(h - x0)
                    cx_scale(h - x0)
                if h == GATED["x"] - 1:
                    for i in range(4):
                        dve.wait_ge(s["ox_hi"], i + 1)
                        dve.tensor_tensor(Q_lo[:, 2 * i:2 * i + 2, :], ox[:, 2 * i:2 * i + 2, :],
                                          Q_hi[:, 2 * i:2 * i + 2, :].bitcast(F32), ALU.subtract)\
                           .then_inc(s["ox_lo"], 1)
                if h + 4 < FFN1 + 2:
                    split(0, h + 4)
            rms_norm(2, X, B1, R_hi, R_lo, par[:, G_MLP:G_MLP + KT])
            ffn(0, FFN1, 0)
            for q in range(4):
                if q == 2:
                    dve.wait_ge(s["acc_ready"], 1)
                else:
                    dve.wait_ge(s["gemm_done"], HALVES1 - 1 + (q == 3))
                t = X[:, 2 * q:2 * q + 2, :]
                dve.tensor_tensor(t, t, two(aps[:, q, :]), ALU.add).then_inc(s["resid"], 1)
            for a in range(2):
                split(HALVES1, LF + a, n=32)
            for q in range(4):
                dve.wait_ge(s["nhi"], 12 + q + 1)
                dve.tensor_tensor(H_lo[:, 2 * q:2 * q + 2, :], X[:, 2 * q:2 * q + 2, :],
                                  H_hi[:, 2 * q:2 * q + 2, :].bitcast(F32), ALU.subtract)\
                   .then_inc(s["nlo"], 1)
            dve.wait_ge(s["con_loaded"], 16)

            with dve.Fori(0, LAYERS) as ly:
                st = Steps(dve, s["dve_step2"], ly * DVE_STEPS_LAYER)
                h0 = ly * HALVES2 + HALVES1
                e0 = ly * EVACS2 + EVACS1
                f0 = ly * 8
                logf = fgate[:, 1, :]

                def forget(h):
                    if h >= 1:
                        dve.wait_ge(s["fx_s"], f0 + h)
                    m = fm[:, h % 2, :]
                    dve.tensor_scalar(m[:, 0:256], le_one, logf[:, h:h + 1], None, ALU.mult)
                    dve.tensor_scalar(m[:, 256:384], le, logf[:, 8 + h:9 + h], None, ALU.mult)\
                       .then_inc(s["f_m"], 1)

                def fox_max(h):
                    dve.wait_ge(s["fx_s"], f0 + (h + 1))
                    if h >= 2:
                        dve.wait_ge(s["fx_t"], f0 + (h - 1))
                    lg = fl[:, h % 2, :]
                    dve.tensor_tensor(lg, aps[:, h % 2, 0:384], causal, ALU.add).then_inc(s["fx_l"], 1)
                    dve.wait_ge(s["fx_l"], f0 + (h + 1))
                    dve.tensor_reduce(small[:, 3, 2 * h:2 * h + 1], lg[:, 0:128], AX.X, ALU.max)
                    st.mark(dve.tensor_reduce(small[:, 3, 2 * h + 1:2 * h + 2], lg[:, 128:384],
                                              AX.X, ALU.max))
                    st.settle()
                    dve.tensor_scalar(small[:, 1, 2 * h:2 * h + 2], small[:, 3, 2 * h:2 * h + 2],
                                      -1.0, None, ALU.mult).then_inc(s["fx_max"], 1)

                def fox_scale(h):
                    dve.wait_ge(s["fx_e"], ly * 16 + (2 * h + 2))
                    lg = fl[:, h % 2, :]
                    st.mark(dve.reciprocal(small[:, 3, 2 * h:2 * h + 2], small[:, 2, 2 * h:2 * h + 2]))
                    st.settle()
                    dve.tensor_scalar(lg[:, 0:128], lg[:, 0:128], small[:, 3, 2 * h:2 * h + 1],
                                      None, ALU.mult)
                    dve.tensor_scalar(lg[:, 128:384], lg[:, 128:384], small[:, 3, 2 * h + 1:2 * h + 2],
                                      None, ALU.mult).then_inc(s["fx_p"], 1)

                def fox_out(c):
                    dve.wait_ge(s["fx_ohi"], ly * 4 + (c + 1))
                    dve.tensor_tensor(Q_lo[:, c, :], aps[:, 3, 0:T], Q_hi[:, c, :].bitcast(F32),
                                      ALU.subtract).then_inc(s["fx_oe"], 1)

                def rotate(r):
                    x = (rq if r < 2 else rk)[:, 2 * (r % 2):2 * (r % 2) + 2, :]
                    dve.wait_ge(s["rt_mm"], ly * 4 + (r + 1))
                    st.mark(dve.tensor_tensor(rott, two(gps[:, 3, :]), sin_b, ALU.mult))
                    st.mark(dve.tensor_tensor(x, x, cos_b, ALU.mult))
                    st.settle()
                    dve.tensor_tensor(x, x, rott, ALU.add).then_inc(s["rt_x"], 1)

                for l in range(LFFN):
                    if l == LFK:
                        dve.wait_ge(s["f_gate"], ly + 1)
                        dve.wait_ge(s["lpar_loaded"], ly * 16 + 16)
                        fg = fgate[:, 0, :].rearrange("p (a h) -> p a h", a=2)
                        dve.tensor_tensor(fg, fg, lpar[:, B_F:B_F + 8].unsqueeze(1).to_broadcast([P, 2, 8]),
                                          ALU.add).then_inc(s["f_logit"], 1)
                        dve.wait_ge(s["f_logit"], ly + 1)
                        dve.wait_ge(s["f_sp"], ly + 1)
                        st.mark(dve.scalar_tensor_tensor(logf, fgate[:, 0, :], 0.0, small[:, 0, :],
                                                         ALU.min, ALU.subtract))
                        st.settle()
                    if l >= LWO:
                        i = l - LWO
                        if i == 2:
                            first_half(ly * 2, ly * 8 + 8)
                            split(h0, LFFN)
                            shift(ly * 2)
                        dve.wait_ge(s["gemm_done"], h0 + (l + 1))
                        (residual if i < 2 else shifted)(i, two(gps[:, l % 3, :]))
                        if i == 2:
                            shift_first(ly * 2)
                            early_squares(ly * 2)
                        if i == 3:
                            second_half(ly * 2, ly * 8 + 8)
                    if l >= 7 and l <= 14 and l % 2 == 0:
                        fox_out((l - 8) // 2)
                    if l == 4:
                        forget(0)
                    if 5 <= l < 13:
                        fox_max(l - 5)
                        if l < 12:
                            forget(l - 4)
                        fox_scale(l - 5)
                    if 9 <= l < 13:
                        rotate(l - 9)
                    if l in (LRG - 1, LRG):
                        for h in (range(3) if l < LRG else (3,)):
                            sc = retention_bank(h)
                            dve.wait_ge(s["rn_s"], ly * 4 + (h + 1))
                            dve.tensor_tensor(inner[:, h, 0:256], sc[:, 0:256], decay[:, h, :], ALU.mult)
                            dve.tensor_tensor(inner[:, h, 256:384], sc[:, 256:384], decay[:, h, 0:128],
                                              ALU.mult).then_inc(s["rn_m"], 1)
                    if l + 4 < LWO + 3:
                        split(h0, l + 4)
                    if l == LRG + 1:
                        def centre(b):
                            t = ro[:, 2 * b:2 * b + 2, :]
                            dve.wait_ge(s["gn_mean"], ly * 2 + (b + 1))
                            dve.scalar_tensor_tensor(t, two(aps[:, 2 + b, :]), -1.0 / P, t, ALU.mult,
                                                     ALU.add).then_inc(s["gn_c"], 1)

                        centre(0)
                        dve.wait_ge(s["evac"], e0 + LWO - 1)
                        for h in range(RET_HEADS):
                            ins = dve.scalar_tensor_tensor(rg[:, h, :], rg[:, h, :],
                                                           lpar[:, GN_G + h:GN_G + h + 1], rsig[:, h, :],
                                                           ALU.mult, ALU.mult)
                        st.mark(ins)
                        centre(1)
                        st.settle()
                        dve.wait_ge(s["gn_c"], ly * 2 + 2)
                        st.mark(dve.tensor_tensor(rg, rg, ro, ALU.mult))
                        st.settle()
                        def pair(buf, b):
                            return buf[:, 2 * b:2 * b + 2, :]

                        def gn_root(b):
                            dve.wait_ge(s["gn_v"], ly * 2 + (b + 1))
                            dve.wait_ge(s["gn_log"], ly * 2 + (b + 1))
                            newton(pair(gv, b), pair(gr0, b), pair(ga, b), pair(gv, b), None)

                        def gn_lo(b):
                            dve.wait_ge(s["gn_hi"], ly * 2 + (b + 1))
                            dve.tensor_tensor(Q_lo[:, 4 + 2 * b:6 + 2 * b, :], pair(ro, b),
                                              Q_hi[:, 4 + 2 * b:6 + 2 * b, :].bitcast(F32),
                                              ALU.subtract).then_inc(s["gn_lo"], 1)

                        for b in range(2):
                            dve.wait_ge(s["gn_var"], ly * 2 + (b + 1))
                            dve.tensor_scalar(pair(gv, b), two(aps[:, b, :]), 1.0 / P, EPS_GN,
                                              ALU.mult, ALU.add).then_inc(s["gn_v"], 1)
                            if b == 1:
                                gn_root(0)
                                dve.tensor_tensor(pair(ro, 0), pair(gv, 0), pair(rg, 0), ALU.mult)\
                                   .then_inc(s["gn_y"], 1)
                                dve.wait_ge(s["gn_y"], ly * 2 + 1)
                        gn_lo(0)
                        gn_root(1)
                        dve.tensor_tensor(pair(ro, 1), pair(gv, 1), pair(rg, 1), ALU.mult)\
                           .then_inc(s["gn_y"], 1)
                        dve.wait_ge(s["gn_y"], ly * 2 + 2)
                        gn_lo(1)
                        split(h0, LWO + 3)
                layer_norm(ly * 2, R_hi, R_lo)
                split(h0, LFFN + 1)
                ffn(h0, LFFN, ly * 16 + 16)
                for q in range(4):
                    if q == 2:
                        first_half(ly * 2 + 1, ly * 8 + 12)
                        shift(ly * 2 + 1)
                        dve.wait_ge(s["acc_ready"], ly + 2)
                    else:
                        dve.wait_ge(s["gemm_done"], h0 + (HALVES2 - 1 + (q == 3)))
                    (residual if q < 2 else shifted)(q, two(aps[:, q, :]))
                    if q == 2:
                        shift_first(ly * 2 + 1)
                        early_squares(ly * 2 + 1)
                second_half(ly * 2 + 1, ly * 8 + 12)
                for a in range(2):
                    split(h0, HALVES2 + LF + a, n=32)
                layer_norm(ly * 2 + 1, H_hi, H_lo)
                assert st.n == DVE_STEPS_LAYER, st.n

        @block.tensor
        def _(pe):
            def rows_part(l, bank_, op_hi, op_lo, nts, ks, split_count=None):
                r = ring(l)

                def product(w, op, k, nt, start=False, stop=False):
                    c = k * 256 + nt * P
                    return pe.matmul(gps[:, bank_, nt * T:(nt + 1) * T], w[:, r, c:c + P], op[:, k, :],
                                     start=start, stop=stop, skip_group_check=True)

                for k in ks:
                    if k % 2:
                        continue
                    pair = [(k + j, nt) for nt in nts for j in range(2)]
                    if split_count is not None:
                        pe.wait_ge(split_count[0], split_count[2] + (k // 2 + 1))
                    for kk, nt in pair:
                        product(w_hi, op_hi, kk, nt, start=(kk == 0 and nt == 0))
                        product(w_lo, op_hi, kk, nt)
                    if split_count is not None:
                        pe.wait_ge(split_count[1], split_count[2] + (k // 2 + 1))
                    for kk, nt in pair:
                        ins = product(w_hi, op_lo, kk, nt, stop=(kk == KT - 1 and nt == 1))
                return ins

            def rows_first(h0, l, bank_, op_hi, op_lo, split_count=None):
                pe.wait_ge(s["lo_ready"], h0 + (l + 1))
                if split_count is not None:
                    ins = rows_part(l, bank_, op_hi, op_lo, range(2), range(KT), split_count)
                else:
                    for nt in range(2):
                        ins = rows_part(l, bank_, op_hi, op_lo, (nt,), range(KT))
                ins.then_inc(s["gemm_done"], 1)

            def tokens_first(h0, l, bank_, op_hi, op_lo):
                pe.wait_ge(s["lo_ready"], h0 + (l + 1))
                r = ring(l)
                for m in range(2):
                    for k in range(KT):
                        out = gps[:, bank_, m * 256:(m + 1) * 256]
                        wh, wl = w_hi[:, r, k * 256:(k + 1) * 256], w_lo[:, r, k * 256:(k + 1) * 256]
                        xh, xl = op_hi[:, k, m * P:(m + 1) * P], op_lo[:, k, m * P:(m + 1) * P]
                        pe.matmul(out, xh, wh, start=(k == 0), stop=False)
                        pe.matmul(out, xh, wl, start=False, stop=False)
                        ins = pe.matmul(out, xl, wh, start=False, stop=(k == KT - 1))
                ins.then_inc(s["gemm_done"], 1)

            def sum_tiles(src, tiles, out, start, stop):
                for k in tiles:
                    ins = pe.matmul(out, ones, src[:, k, 0:T], start=(start and k == tiles[0]),
                                    stop=(stop and k == tiles[-1]))
                return ins

            def first_mean(n):
                pe.wait_ge(s["lpre"], n + 1)
                sum_tiles(B1, (0, 1), gps[:, 3, 0:T], True, True).then_inc(s["lmean"], 1)

            def layer_norm(n):
                pe.wait_ge(s["lsq"], n * 3 + 1)
                sum_tiles(B5, (4, 5), aps[:, 0, 0:T], True, False)
                pe.wait_ge(s["lpsq"], n + 1)
                sum_tiles(B5, (0, 1), aps[:, 0, 0:T], False, False)
                pe.wait_ge(s["lshift"], n + 1)
                sum_tiles(B1, (0, 1), gps[:, 3, T:2 * T], True, True).then_inc(s["lsum"], 1)
                pe.wait_ge(s["lsq"], n * 3 + 3)
                sum_tiles(B5, (6, 7), aps[:, 0, 0:T], False, True).then_inc(s["nsum"], 1)

            def ffn(h0, l0, ub, split_count, ln=None):
                def up(h, l, par_, free_sem, free_count):
                    for a in range(2):
                        pe.wait_ge(free_sem, free_count + a)
                        rows_first(h, l + a, 2 * par_ + a, R_hi, R_lo,
                                   split_count if free_sem is not s["ffn_relu"] else None)

                def down(h, l, par_, uu, first=False, last=False):
                    pe.wait_ge(s["hidden"], uu)
                    for a in range(2):
                        pe.wait_ge(s["lo_ready"], h + (l + a + 1))
                        r = ring(l + a)
                        for nt in range(4):
                            if last and a == 1 and nt == 2:
                                ins.then_inc(s["acc_ready"], 1)
                                if ln is not None:
                                    first_mean(ln)
                            out = aps[:, 2 * a + nt // 2, (nt % 2) * T:(nt % 2 + 1) * T]
                            for k in range(4):
                                c = k * 512 + nt * P
                                hh, hl = Q_hi[:, 4 * par_ + k, :], Q_lo[:, 4 * par_ + k, :]
                                pe.matmul(out, w_hi[:, r, c:c + P], hh,
                                          start=(first and k == 0 and nt % 2 == 0), stop=False,
                                          skip_group_check=True)
                                pe.matmul(out, w_hi[:, r, c:c + P], hl, start=False, stop=False,
                                          skip_group_check=True)
                                ins = pe.matmul(out, w_lo[:, r, c:c + P], hh, start=False,
                                                stop=(last and k == 3 and nt % 2 == 1),
                                                skip_group_check=True)
                        ins.then_inc(s["gemm_done"], 1)

                relu = s["ffn_relu"]
                for a in range(2):
                    rows_first(h0, l0 + a, a, R_hi, R_lo, split_count if a == 0 else None)
                for a in range(2):
                    rows_first(h0, l0 + 2 + a, 2 + a, R_hi, R_lo)
                down(h0, l0 + 4, 0, ub + 2, first=True)
                with pe.Fori(0, 3) as f:
                    hf, uf = h0 + f * 8, ub + f * 4
                    up(hf, l0 + 6, 0, relu, uf + 1)
                    down(hf, l0 + 8, 1, uf + 4)
                    up(hf, l0 + 10, 1, relu, uf + 3)
                    down(hf, l0 + 12, 0, uf + 6)
                down(h0, l0 + 30, 1, ub + 16, last=True)

            def sb_scores(i):
                if i >= 1:
                    pe.wait_ge(s["sb_lb"], i)
                for hh in range(2):
                    q, k = qs[64 * hh:64 * hh + 64, i, :], ks[64 * hh:64 * hh + 64, i, :]
                    pe.matmul(aps[:, hh, 0:256], k[:, 0:128], q, start=True, stop=True)
                    ins = pe.matmul(aps[:, hh, 256:384], k[:, 128:256], q[:, 128:256],
                                    start=True, stop=True)
                ins.then_inc(s["sb_z"], 1)

            def sb_between(i):
                pe.wait_ge(s["sb_soft"], i + 1)
                if i >= 1:
                    pe.wait_ge(s["sb_arg"], i)
                for hh in range(2):
                    pe.matmul(aps[:, 2 + hh, 0:384], gt, soft[:, hh, :], start=True, stop=False)
                    ins = pe.matmul(aps[:, 2 + hh, 128:256], ones, soft[:, hh, 256:384],
                                    start=False, stop=True)
                ins.then_inc(s["sb_t"], 1)

            def sb_values(i):
                pe.wait_ge(s["sb_a"], i + 1)
                if i >= 1:
                    pe.wait_ge(s["sb_olo"], i)
                for hh in range(2):
                    c = (2 * i + hh) * 64
                    a = spb[:, i % 2, hh, :]
                    out = gps[64 * hh:64 * hh + 64, 3, :]
                    pe.matmul(out[:, 0:256], vs[:, 0, c:c + 64], a[:, 0:256], start=True, stop=False)
                    ins = pe.matmul(out[:, 128:256], vs[:, 1, c:c + 64], a[:, 256:384],
                                    start=False, stop=True)
                ins.then_inc(s["sb_o"], 1)

            def head_sum(n):
                pe.wait_ge(s["hsq"], n + 1)
                if n == 0:
                    pe.wait_ge(s["sb_olo"], SB_PAIRS)
                else:
                    pe.wait_ge(s["hn_row"], n)
                for j in range(2):
                    ins = pe.matmul(gps[:, 3, 0:T], ones, sqh[:, n % 2, j * T:(j + 1) * T],
                                    start=(j == 0), stop=(j == 1))
                ins.then_inc(s["hn_sum"], 1)

            def cx_scores(h):
                pe.wait_ge(s["hn_norm"], 4 + h + 1)
                if h >= 2:
                    pe.wait_ge(s["cx_exp"], 2 * (h - 1))
                for t in range(2):
                    for j in range(2):
                        ins = pe.matmul(aps[:, h % 2, t * T:(t + 1) * T],
                                        qx[:, 2 * h + j, t * P:(t + 1) * P], kx[:, 2 * h + j, :],
                                        start=(j == 0), stop=(j == 1))
                ins.then_inc(s["cx_s"], 1)

            def cx_transpose(h):
                pe.wait_ge(s["cx_p"], h + 1)
                if h >= 1:
                    pe.wait_ge(s["cx_pt"], h)
                for m in range(2):
                    for t in range(2):
                        ins = pe.transpose(aps[:, 3, m * T + t * P:m * T + (t + 1) * P],
                                           xp[:, t, m * P:(m + 1) * P], ident)
                ins.then_inc(s["cx_t"], 1)

            def cx_values(h):
                pe.wait_ge(s["cx_pt"], h + 1)
                if h >= 1:
                    pe.wait_ge(s["cx_oe"], h)
                for j in range(2):
                    for m in range(2):
                        c = h * 256 + j * P
                        ins = pe.matmul(aps[:, 2, j * T:(j + 1) * T], vx[:, m, c:c + P],
                                        xpt[:, m * T:(m + 1) * T], start=(m == 0), stop=(m == 1))
                ins.then_inc(s["cx_o"], 1)

            pe.wait_ge(s["par_loaded"], 32)
            pe.wait_ge(s["sqsum"], 1)
            sum_tiles(B5, (0, 1), aps[:, 3, 0:T], True, True).then_inc(s["nsum"], 1)
            for h in range(FFN1):
                if h - 3 >= WO1:
                    pe.wait_ge(s["resid"], h - 3 - WO1 + 1)
                elif h >= 3:
                    pe.wait_ge(s["evac"], h - 2)
                if h < SV:
                    rows_first(0, h, h % 3, H_hi, H_lo, (s["nhi"], s["nlo"], 0) if h == 0 else None)
                elif h < CC:
                    tokens_first(0, h, h % 3, H_hi, H_lo)
                elif h < MK or XQ <= h < XQ + 4:
                    rows_first(0, h, h % 3, H_hi, H_lo)
                elif h < MV:
                    rows_first(0, h, h % 3, R_hi, R_lo, (s["nhi"], s["nlo"], 4) if h == MK else None)
                elif h < XQ:
                    tokens_first(0, h, h % 3, R_hi, R_lo)
                elif h < WO1:
                    if (h - 36) % 2 == 0:
                        rows_first(0, h, h % 3, H_hi, H_lo)
                    elif h < GATED["x"]:
                        if h == GATED["sb"] + 1:
                            pe.wait_ge(s["sb_olo"], SB_PAIRS)
                        rows_first(0, h, h % 3, Q_hi, Q_lo)
                    elif h < GATED["conv"]:
                        rows_first(0, h, h % 3, Q_hi, Q_lo, (s["ox_hi"], s["ox_lo"], 0) if h == GATED["x"] + 1 else None)
                    else:
                        if h == GATED["conv"] + 1:
                            pe.wait_ge(s["cv_lo"], 4)
                        rows_first(0, h, h % 3, R_hi, R_lo)
                else:
                    rows_first(0, h, h % 3, Q_hi, Q_lo, (s["mg_hi"], s["mg_lo"], 0) if h == WO1 else None)
                if h == MEM0 + 2:
                    pe.wait_ge(s["nrow"], 1)
                    pe.wait_ge(s["sqsum"], 2)
                    sum_tiles(B5, (0, 1), aps[:, 3, 0:T], True, True).then_inc(s["nsum"], 1)
                if SB0 <= h <= SB0 + 18 and h % 2 == 0:
                    t = (h - SB0) // 2
                    if t == 2:
                        pe.wait_ge(s["evac"], CC)
                    if t >= 2:
                        sb_values(t - 2)
                    if t < SB_PAIRS:
                        if t == 0:
                            pe.wait_ge(s["evac"], SV)
                            pe.wait_ge(s["nrow"], 2)
                        sb_scores(t)
                    if 1 <= t <= SB_PAIRS:
                        sb_between(t - 1)
                if HN0 <= h < HN0 + 8:
                    head_sum(h - HN0)
                x0 = XQ + 3
                if x0 + 2 <= h < x0 + 2 + X_HEADS:
                    cx_values(h - x0 - 2)
                if x0 + 1 <= h < x0 + 1 + X_HEADS:
                    cx_transpose(h - x0 - 1)
                if x0 <= h < x0 + X_HEADS:
                    cx_scores(h - x0)
            pe.wait_ge(s["sqsum"], 3)
            sum_tiles(B5, (0, 1), aps[:, 3, 0:T], True, False)
            pe.wait_ge(s["nsq"], 8)
            sum_tiles(B5, (6, 7), aps[:, 3, 0:T], False, True).then_inc(s["nsum"], 1)
            pe.wait_ge(s["resid"], 4)
            pe.wait_ge(s["nrow"], 3)
            ffn(0, FFN1, 0, (s["nhi"], s["nlo"], 8))

            pe.wait_ge(s["con_loaded"], 16)
            with pe.Fori(0, LAYERS) as ly:
                h0 = ly * HALVES2 + HALVES1
                e0 = ly * EVACS2 + EVACS1
                f0 = ly * 8

                def fox_scores(h):
                    pe.wait_ge(s["f_m"], f0 + (h + 1))
                    if h >= 2:
                        pe.wait_ge(s["fx_l"], f0 + (h - 1))
                    q = fq[64 * (h % 2):64 * (h % 2) + 64, h // 2, :]
                    k = fk[64 * (h % 2):64 * (h % 2) + 64, h // 2, :]
                    m = fm[:, h % 2, :]
                    o = aps[:, h % 2, :]
                    pe.matmul(o[:, 0:128], q[:, 0:128], k[:, 0:128], start=True, stop=False)
                    pe.matmul(o[:, 0:128], m[:, 0:128], gt, start=False, stop=True)
                    pe.matmul(o[:, 128:384], q[:, 128:256], k, start=True, stop=False)
                    pe.matmul(o[:, 128:256], m[:, 128:256], gt, start=False, stop=False)
                    pe.matmul(o[:, 128:256], m[:, 256:384], ones, start=False, stop=False)
                    pe.matmul(o[:, 256:384], m[:, 256:384], gt, start=False, stop=True)\
                      .then_inc(s["fx_s"], 1)

                def fox_transpose(h):
                    pe.wait_ge(s["fx_p"], f0 + (h + 1))
                    if h >= 1:
                        pe.wait_ge(s["fx_pt"], f0 + h)
                    for c in range(3):
                        ins = pe.transpose(aps[:, 2, c * P:(c + 1) * P],
                                           fl[:, h % 2, c * P:(c + 1) * P], ident)
                    ins.then_inc(s["fx_t"], 1)

                def fox_values(h):
                    pe.wait_ge(s["fx_pt"], f0 + (h + 1))
                    if h % 2 == 0 and h >= 2:
                        pe.wait_ge(s["fx_oe"], ly * 4 + h // 2)
                    o = aps[64 * (h % 2):64 * (h % 2) + 64, 3, :]
                    pt = fpt[:, h % 2, :]
                    pe.matmul(o[:, 0:256], fv[:, 0, 64 * h:64 * h + 64], pt[:, 0:256],
                              start=True, stop=False)
                    pe.matmul(o[:, 128:256], fv[:, 1, 64 * h:64 * h + 64], pt[:, 256:384],
                              start=False, stop=True).then_inc(s["fx_o"], 1)

                def rotate(r):
                    x = (rq if r < 2 else rk)[:, 2 * (r % 2):2 * (r % 2) + 2, :]
                    if r >= 1:
                        pe.wait_ge(s["rt_x"], ly * 4 + r)
                    pe.wait_ge(s["evac"], e0 + (LRQ + r))
                    pe.matmul(gps[:, 3, :], rot, x, start=True, stop=True).then_inc(s["rt_mm"], 1)

                def retention_values(b):
                    pe.wait_ge(s["rn_m"], ly * 4 + 2 * b + 2)
                    for h in (2 * b, 2 * b + 1):
                        o = aps[:, b, (h % 2) * T:(h % 2 + 1) * T]
                        pe.matmul(o, rv[:, 0, h * P:(h + 1) * P], inner[:, h, 0:256],
                                  start=True, stop=False)
                        ins = pe.matmul(o[:, 128:256], rv[:, 1, h * P:(h + 1) * P],
                                        inner[:, h, 256:384], start=False, stop=True)
                    ins.then_inc(s["rn_o"], 1)

                def retention_mean(b):
                    pe.wait_ge(s["rn_m"], ly * 4 + 4)
                    pe.wait_ge(s["fx_oe"], ly * 4 + 4)
                    pe.wait_ge(s["rn_oe"], ly * 2 + (b + 1))
                    pe.matmul(aps[:, 2 + b, :], ones, ro[:, 2 * b:2 * b + 2, :],
                              start=True, stop=True).then_inc(s["gn_mean"], 1)

                def retention_variance(b):
                    pe.wait_ge(s["gn_sq"], ly * 2 + (b + 1))
                    pe.matmul(aps[:, b, :], ones, gsq[:, 2 * b:2 * b + 2, :],
                              start=True, stop=True).then_inc(s["gn_var"], 1)

                def w_out_part(l, part):
                    if part == 0:
                        pe.wait_ge(s["lo_ready"], h0 + (l + 1))
                        pe.wait_ge(s["evac"], e0 + (l - 3))
                    ks = (range(4), (4, 5), (6, 7))[part]
                    ins = rows_part(l, l % 3, Q_hi, Q_lo, range(2), ks,
                                    None if part == 0 else (s["gn_hi"], s["gn_lo"], ly * 2 - 2))
                    if part == 2:
                        ins.then_inc(s["gemm_done"], 1)

                pe.wait_ge(s["ffn_relu"], ly * 16 + 16)
                pe.wait_ge(s["resid"], ly * 8 + 8)
                for l in range(LFFN):
                    if l >= LWO + 3:
                        pe.wait_ge(s["resid"], ly * 8 + (8 + l - 3 - LWO + 1))
                    elif 4 <= l < LWO:
                        pe.wait_ge(s["evac"], e0 + (l - 3 if l > LFK + 1 else l - 2))
                    b = l % 3
                    if LF <= l < LFK:
                        pe.wait_ge(s["lo_ready"], h0 + (l + 1))
                        r = ring(l)
                        o = gps[0:FOX_HEADS, LF % 3, 0:T]
                        for k in range(4):
                            kk = 4 * (l - LF) + k
                            wh, wl = w_hi[:, r, k * 8:k * 8 + 8], w_lo[:, r, k * 8:k * 8 + 8]
                            pe.matmul(o, wh, H_hi[:, kk, :], start=(kk == 0), stop=False)
                            pe.matmul(o, wh, H_lo[:, kk, :], start=False, stop=False)
                            ins = pe.matmul(o, wl, H_hi[:, kk, :], start=False, stop=(kk == KT - 1))
                        ins.then_inc(s["gemm_done"], 1)
                    elif l < LFV or LRQ <= l < LRV or LRG <= l < LWO:
                        rows_first(h0, l, b, H_hi, H_lo, (s["nhi"], s["nlo"], ly * 8 + 12) if l == 0 else None)
                    elif l < LRG:
                        tokens_first(h0, l, b, H_hi, H_lo)
                    elif l == LWO + 3:
                        pe.wait_ge(s["lo_ready"], h0 + (l + 1))
                        rows_part(l, b, Q_hi, Q_lo, (0,), range(KT))
                        first_mean(ly * 2)
                        rows_part(l, b, Q_hi, Q_lo, (1,), range(KT)).then_inc(s["gemm_done"], 1)
                    if l == LFK:
                        pe.wait_ge(s["evac"], e0 + 3)
                        for m in range(2):
                            ins = pe.matmul(gps[:, 3, m * 8:m * 8 + 8], gate_rows[:, m * P:(m + 1) * P],
                                            ident[0:FOX_HEADS, 0:FOX_HEADS], start=True, stop=True)
                        ins.then_inc(s["f_cols"], 1)
                    if 7 <= l < 15:
                        if l == 7:
                            pe.wait_ge(s["evac"], e0 + LFV)
                        if l == 11:
                            pe.wait_ge(s["evac"], e0 + (LFV + 1))
                        fox_values(l - 7)
                    if 6 <= l < 14:
                        fox_transpose(l - 6)
                    if 5 <= l < 13:
                        if l == 5:
                            pe.wait_ge(s["evac"], e0 + LFK)
                        if l == 9:
                            pe.wait_ge(s["evac"], e0 + (LFK + 1))
                        fox_scores(l - 5)
                    if 9 <= l < 13:
                        rotate(l - 9)
                    if l in (LRG - 1, LRG):
                        if l < LRG:
                            pe.wait_ge(s["rt_x"], ly * 4 + 4)
                            pe.wait_ge(s["fx_l"], f0 + 8)
                        else:
                            pe.wait_ge(s["fx_pt"], f0 + 8)
                        for h in (range(3) if l < LRG else (3,)):
                            sc = retention_bank(h)
                            pe.matmul(sc[:, 0:256], rk[:, h, 0:128], rq[:, h, :], start=True, stop=True)
                            pe.matmul(sc[:, 256:384], rk[:, h, 128:256], rq[:, h, 128:256],
                                      start=True, stop=True).then_inc(s["rn_s"], 1)
                    if l == LRG:
                        retention_values(0)
                    if l == LRG + 1:
                        retention_mean(0)
                        retention_values(1)
                        w_out_part(LWO, 0)
                        retention_mean(1)
                        retention_variance(0)
                        w_out_part(LWO + 1, 0)
                        retention_variance(1)
                        w_out_part(LWO + 2, 0)
                        for part in (1, 2):
                            for i in range(3):
                                w_out_part(LWO + i, part)
                layer_norm(ly * 2)
                pe.wait_ge(s["nrow"], ly * 2 + 4)
                ffn(h0, LFFN, ly * 16 + 16, (s["nhi"], s["nlo"], ly * 8 + 16), ln=ly * 2 + 1)
                layer_norm(ly * 2 + 1)


def shape_constants():
    i = np.arange(P)
    c1 = np.zeros((P, CONSTS1), np.float32)
    c1[:, C_ID:C_ID + P] = np.eye(P)
    c1[:, C_GT:C_GT + P] = i[:, None] > i[None, :]
    c1[:, C_LE:C_LE + P] = i[:, None] <= i[None, :]
    c1[:, C_ONE:C_ONE + P] = 1.0
    c1[:, C_PAST:C_PAST + P] = i[:, None] < i[None, :]
    c2 = np.zeros((P, CONSTS2), np.float32)
    half = P // 2
    inv = np.float32(10000.0) ** (-np.arange(half, dtype=np.float32) / np.float32(half))
    ang = np.arange(T, dtype=np.float32)[None, :] * inv[:, None]
    c2[:, C_COS:C_COS + T] = np.tile(np.cos(ang), (2, 1))
    c2[:, C_SIN:C_SIN + T] = np.tile(np.sin(ang), (2, 1))
    log_g = np.log(1.0 - 2.0 ** (-5.0 - np.arange(RET_HEADS)))
    diff = np.arange(T)[None, :] - i[:, None]
    for h in range(RET_HEADS):
        c2[:, C_DECAY + h * T:C_DECAY + (h + 1) * T] = np.where(
            diff >= 0, np.exp(log_g[h] * np.maximum(diff, 0)), 0.0)
    for d in range(half):
        c2[d + half, C_ROT + d] = -1.0
        c2[d, C_ROT + d + half] = 1.0
    block = np.where(i[None, :] <= i[:, None], 0.0, -3.0e38)
    c2[:, C_CAUSAL:C_CAUSAL + P] = block
    c2[:, C_CAUSAL + 2 * P:C_CAUSAL + 3 * P] = block
    return c1, c2


def kernel(**inputs):
    import concourse.bacc as bacc
    from concourse.bass_utils import run_bass_kernel_spmd as run

    a = {k: np.ascontiguousarray(v) for k, v in inputs.items()}

    def halves(w):
        j = w.shape[1] // 256
        return w.reshape(KT, P, j, 256).transpose(2, 1, 0, 3).reshape(j, P, HALF)

    def down_halves(w):
        return w.reshape(8, 4, P, 2, 512).transpose(0, 3, 2, 1, 4).reshape(16, P, HALF)

    def mlp_order(up, down):
        u, d = halves(up), down_halves(down)
        parts = [u[0:2], u[2:4], d[0:2]]
        for j in range(2, 8):
            parts += [u[2 * j:2 * j + 2], d[2 * j - 2:2 * j]]
        return parts + [d[14:16]]

    def pairs(g, w):
        return [x[i:i + 1] for i in range(4) for x in (g, w)]

    win, kv = a["w_in"][0], a["w_mem_kv"][0]
    col = [halves(win[:, i * D:(i + 1) * D]) for i in range(10)]
    c_h, c_b, c_c, sq, sk, sv, xq, g0, g1, g2 = col
    w1 = np.concatenate(
        [sq, sk, sv, c_c, c_h, c_b, halves(kv[:, :D]), halves(kv[:, D:]), xq]
        + pairs(g1, halves(a["w_sb_out"][0])) + pairs(g2, halves(a["w_x_out"][0]))
        + pairs(g0, halves(a["w_conv_out"][0])) + [halves(a["w_out"][0])]
        + mlp_order(a["w_up"][0], a["w_down"][0]))
    w2, wf = [], []
    for ly in range(LAYERS):
        w = a["w_in_2"][ly]
        w2.append(np.concatenate(
            [halves(w[:, :1536]), halves(w[:, 1544:]), halves(a["w_out_2"][ly])]
            + mlp_order(a["w_ff1_2"][ly], a["w_ff2_2"][ly])))
        wf.append(w[:, 1536:1544].reshape(2, 4, P, 8).transpose(0, 2, 1, 3).reshape(2, P, 32))

    w2 = np.concatenate(w2 + [w2[0][0:2]])
    wf.append(wf[0])

    def cols(v):
        return v.reshape(-1, P).T

    par1 = np.concatenate([cols(a[n]) for n in ("g_mix", "g_mem", "g_mlp", "q_norm_g", "k_norm_g")]
                          + [cols(a["conv_w"][0, j]) for j in range(3)], axis=1)
    par2 = np.stack([np.concatenate(
        [cols(a[n][ly]) for n in ("ln1_g_2", "ln1_b_2", "ln2_g_2", "ln2_b_2", "ret_gn_g_2")]
        + [np.broadcast_to(a["b_forget_2"][ly], (P, FOX_HEADS))], axis=1) for ly in range(LAYERS)])
    con1, con2 = shape_constants()
    arrays = {"mem_t": a["mem"][0].T, "x_t": a["x"][0].T, "w1": w1, "w2": w2,
              "wf": np.stack(wf), "par1": par1, "par2": par2, "con1": con1, "con2": con2}
    arrays = {k: np.ascontiguousarray(v) for k, v in arrays.items()}
    nc = bacc.Bacc("TRN2", target_bir_lowering=False, num_devices=1)
    args = [nc.dram_tensor(k, v.shape, mybir.dt.from_np(v.dtype), kind="ExternalInput").ap()
            for k, v in arrays.items()]
    out = nc.dram_tensor("out_t", (D, T), F32, kind="ExternalOutput").ap()
    build(nc, *args, out)
    r = run(nc, [arrays], core_ids=[0])
    return np.ascontiguousarray(r.results[0]["out_t"].T).reshape(1, T, D)
```
